# Optimizing a Trainium2 kernel written in Bass

```python
import jax, jax.numpy as jnp
from jax import lax
import numpy as np

D_MODEL = 1024
BATCH = 1
SEQ = 512
DEPTH = 2

CHUNK = 64
N_A_LAYERS = DEPTH // 2
N_B_LAYERS = DEPTH - N_A_LAYERS
D_FF = 2816
D_RNN = D_MODEL
LRU_BLOCKS = 4
LRU_BLOCK_W = D_RNN // LRU_BLOCKS
CONV_WIDTH = 4
LRU_C = 8.0
N_HEADS = 16
N_KV_HEADS = 2
HEAD_DIM = 64
Q_PER_KV = N_HEADS // N_KV_HEADS
WINDOW = 128
WINDOW_CHUNKS = WINDOW // CHUNK
BAND = WINDOW_CHUNKS * CHUNK
ROPE_THETA = 500000.0
ROPE_DIM = HEAD_DIM // 4
EPS = 1e-6
MASK_VALUE = -1e30

kernel_name = "yoco_rglru_swa_sink_macaron"

def rmsnorm(x, g):
    xf = x.astype(jnp.float32)
    y = xf * lax.rsqrt(jnp.mean(xf * xf, axis=-1, keepdims=True) + EPS)
    return (y * g.astype(jnp.float32)).astype(x.dtype)

def swiglu(x, w_gu, w_down):
    g, u = jnp.split(x @ w_gu, 2, axis=-1)
    return (jax.nn.silu(g) * u) @ w_down

def partial_rope(x, pos):
    xf = x.astype(jnp.float32)
    rot, keep = xf[..., :ROPE_DIM], xf[..., ROPE_DIM:]
    inv_freq = jnp.power(jnp.float32(ROPE_THETA), -jnp.arange(0, ROPE_DIM, 2, dtype=jnp.float32) / ROPE_DIM)
    ang = pos.astype(jnp.float32)[:, None] * inv_freq[None, :]
    cos, sin = jnp.cos(ang)[None, :, None, :], jnp.sin(ang)[None, :, None, :]
    x1, x2 = jnp.split(rot, 2, axis=-1)
    out = jnp.concatenate([x1 * cos - x2 * sin, x2 * cos + x1 * sin, keep], axis=-1)
    return out.astype(x.dtype)

def rg_lru_block(h, w_in, conv_w, conv_b, gate_w, gate_b, a_param, w_out):
    B, S, _ = h.shape
    xb, yb = jnp.split(h @ w_in, 2, axis=-1)
    gate = jax.nn.gelu(yb)
    xpad = jnp.pad(xb, ((0, 0), (CONV_WIDTH - 1, 0), (0, 0)))
    xc = conv_b
    for k in range(CONV_WIDTH):
        xc = xc + xpad[:, k:k + S] * conv_w[k]
    xblk = xc.reshape(B, S, LRU_BLOCKS, LRU_BLOCK_W)
    gates = jnp.einsum('bshi,ghij->gbshj', xblk, gate_w).reshape(2, B, S, D_RNN) + gate_b[:, None, None, :]
    r = jax.nn.sigmoid(gates[0].astype(jnp.float32))
    i = jax.nn.sigmoid(gates[1].astype(jnp.float32))
    log_a = -LRU_C * r * jax.nn.softplus(-a_param.astype(jnp.float32))
    a = jnp.exp(log_a)
    mult = jnp.sqrt(-jnp.expm1(2.0 * log_a))
    u = mult * (i * xc.astype(jnp.float32))

    def combine(left, right):
        a1, b1 = left
        a2, b2 = right
        return a1 * a2, a2 * b1 + b2

    _, hseq = lax.associative_scan(combine, (a, u), axis=1)
    return (hseq.astype(h.dtype) * gate) @ w_out

def shift_chunks(t, j):
    return jnp.concatenate([jnp.zeros_like(t[:, :j]), t[:, :-j]], axis=1)

def shared_kv(h, kv_norm, w_kv, pos):
    B, S, _ = h.shape
    nc = S // CHUNK
    kv = (rmsnorm(h, kv_norm) @ w_kv).reshape(B, S, 2, N_KV_HEADS, HEAD_DIM)
    k = partial_rope(kv[:, :, 0], pos).reshape(B, nc, CHUNK, N_KV_HEADS, HEAD_DIM)
    v = kv[:, :, 1].reshape(B, nc, CHUNK, N_KV_HEADS, HEAD_DIM)
    k_band = jnp.concatenate([shift_chunks(k, j) for j in range(WINDOW_CHUNKS - 1, 0, -1)] + [k], axis=2)
    v_band = jnp.concatenate([shift_chunks(v, j) for j in range(WINDOW_CHUNKS - 1, 0, -1)] + [v], axis=2)
    chunk_idx = jnp.arange(nc)[:, None] - (WINDOW_CHUNKS - 1 - jnp.arange(WINDOW_CHUNKS))[None, :]
    valid = jnp.repeat(chunk_idx >= 0, CHUNK, axis=1)
    return k_band, v_band, valid

def swa_sink_attention(h, k_band, v_band, valid, w_q, sinks, w_o, pos):
    B, S, _ = h.shape
    nc = S // CHUNK
    q = partial_rope((h @ w_q).reshape(B, S, N_HEADS, HEAD_DIM), pos)
    q = q.reshape(B, nc, CHUNK, N_KV_HEADS, Q_PER_KV, HEAD_DIM)
    scores = jnp.einsum('bnqkgd,bnjkd->bnkgqj', q, k_band).astype(jnp.float32) * (HEAD_DIM ** -0.5)
    scores = jnp.where(valid[None, :, None, None, None, :], scores, MASK_VALUE)
    sink = jnp.broadcast_to(sinks.astype(jnp.float32).reshape(1, 1, N_KV_HEADS, Q_PER_KV, 1, 1),
                            scores.shape[:-1] + (1,))
    p = jax.nn.softmax(jnp.concatenate([scores, sink], axis=-1), axis=-1)[..., :-1].astype(v_band.dtype)
    o = jnp.einsum('bnkgqj,bnjkd->bnqkgd', p, v_band).reshape(B, S, N_HEADS * HEAD_DIM)
    return o @ w_o

def setup_inputs(seed: int = 0) -> dict:
    key = jax.random.key(seed)
    ks = jax.random.split(key, 20)
    f32 = jnp.float32

    def nrm(k, shape, fan_in):
        return jax.random.normal(k, shape, f32) * (fan_in ** -0.5)

    def gain(k, shape):
        return 1.0 + 0.01 * jax.random.normal(k, shape, f32)

    a0 = jax.random.uniform(ks[10], (N_A_LAYERS, D_RNN), f32, 0.9, 0.999)
    return {
        "x": jax.random.normal(ks[0], (BATCH, SEQ, D_MODEL), f32),
        "ffn_norm": gain(ks[1], (DEPTH, 2, D_MODEL)),
        "ffn_w_gu": nrm(ks[2], (DEPTH, 2, D_MODEL, 2 * D_FF), D_MODEL),
        "ffn_w_down": nrm(ks[3], (DEPTH, 2, D_FF, D_MODEL), D_FF),
        "mix_norm": gain(ks[4], (DEPTH, D_MODEL)),
        "lru_w_in": nrm(ks[5], (N_A_LAYERS, D_MODEL, 2 * D_RNN), D_MODEL),
        "lru_conv_w": nrm(ks[6], (N_A_LAYERS, CONV_WIDTH, D_RNN), CONV_WIDTH),
        "lru_conv_b": 0.01 * jax.random.normal(ks[7], (N_A_LAYERS, D_RNN), f32),
        "lru_gate_w": nrm(ks[8], (N_A_LAYERS, 2, LRU_BLOCKS, LRU_BLOCK_W, LRU_BLOCK_W), LRU_BLOCK_W),
        "lru_gate_b": 0.01 * jax.random.normal(ks[9], (N_A_LAYERS, 2, D_RNN), f32),
        "lru_a_param": jnp.log(a0) - jnp.log1p(-a0),
        "lru_w_out": nrm(ks[11], (N_A_LAYERS, D_RNN, D_MODEL), D_RNN),
        "kv_norm": gain(ks[12], (D_MODEL,)),
        "w_kv": nrm(ks[13], (D_MODEL, 2 * N_KV_HEADS * HEAD_DIM), D_MODEL),
        "attn_w_q": nrm(ks[14], (N_B_LAYERS, D_MODEL, N_HEADS * HEAD_DIM), D_MODEL),
        "attn_sinks": 0.5 * jax.random.normal(ks[15], (N_B_LAYERS, N_HEADS), f32),
        "attn_w_o": nrm(ks[16], (N_B_LAYERS, N_HEADS * HEAD_DIM, D_MODEL), N_HEADS * HEAD_DIM),
        "final_norm": gain(ks[17], (D_MODEL,)),
    }

def reference(x, ffn_norm, ffn_w_gu, ffn_w_down, mix_norm, lru_w_in, lru_conv_w, lru_conv_b,
              lru_gate_w, lru_gate_b, lru_a_param, lru_w_out, kv_norm, w_kv, attn_w_q,
              attn_sinks, attn_w_o, final_norm):
    S = x.shape[1]
    pos = jnp.arange(S, dtype=jnp.int32)
    h = x
    k_band = v_band = valid = None
    for layer in range(DEPTH):
        h = h + 0.5 * swiglu(rmsnorm(h, ffn_norm[layer, 0]), ffn_w_gu[layer, 0], ffn_w_down[layer, 0])
        hn = rmsnorm(h, mix_norm[layer])
        if layer < N_A_LAYERS:
            a = layer
            h = h + rg_lru_block(hn, lru_w_in[a], lru_conv_w[a], lru_conv_b[a], lru_gate_w[a],
                                 lru_gate_b[a], lru_a_param[a], lru_w_out[a])
        else:
            b = layer - N_A_LAYERS
            h = h + swa_sink_attention(hn, k_band, v_band, valid, attn_w_q[b], attn_sinks[b],
                                       attn_w_o[b], pos)
        h = h + 0.5 * swiglu(rmsnorm(h, ffn_norm[layer, 1]), ffn_w_gu[layer, 1], ffn_w_down[layer, 1])
        if layer == N_A_LAYERS - 1:
            k_band, v_band, valid = shared_kv(h, kv_norm, w_kv, pos)
    return rmsnorm(h, final_norm)


_drawn_inputs = setup_inputs


def setup_inputs(seed=0):
    import zlib

    import numpy as np

    out = dict(_drawn_inputs(seed))
    spreads = {}
    factors = {'ffn_norm': 6.748,
     'mix_norm': 8.0,
     'lru_conv_b': 3.726,
     'lru_gate_b': 8.0,
     'kv_norm': 31.914,
     'attn_sinks': 8.0,
     'final_norm': 32.96}
    for name, (base, spread) in spreads.items():
        noise = np.random.default_rng([zlib.crc32(name.encode()), seed]).standard_normal(out[name].shape)
        drawn = base * np.exp(spread * noise) if base else spread * noise
        out[name] = __import__('jax').numpy.asarray(drawn.astype(out[name].dtype))
    for name, factor in factors.items():
        out[name] = (out[name] * factor).astype(out[name].dtype)
    return out
```

```python
from contextlib import ExitStack

import numpy as np

import concourse.bass as bass
from concourse import mybir

F32 = mybir.dt.float32
F32R = mybir.dt.float32r
ALU = mybir.AluOpType
ACT = mybir.ActivationFunctionType
AX_X = mybir.AxisListType.X
ds = bass.ds

P = 128
S = 512
D = 1024
DT = D // P
F = 2816
CHUNK = 64
HEAD = 64
KV_HEADS = 2
ROPE = HEAD // 4
THETA = 500000.0
CONV = 4
EPS = 1e-6
MASK = -2.0 ** 100
BLK = DT * P
RAW = 2
RING = 4
BANKS = 4
PARTS = ((0, 6), (6, 8), (14, 8))
assert sum(n for _, n in PARTS) * P == F

V_FFN, V_MIX, V_KV, V_FINAL, V_CONVW, V_CONVB, V_GATEB, V_A = 0, 32, 48, 56, 64, 96, 104, 120

T_ID, T_SWAP, T_DUP, T_DUPSWAP, T_COS, T_SIN, T_END = 0, 128, 256, 512, 768, 1280, 1792


def shape_tables():
    t = np.zeros((P, T_END), np.float32)
    t[np.arange(P), T_ID + np.arange(P)] = 1.0
    half = ROPE // 2
    for m in range(P):
        d = m % HEAD
        mate = d + half if d < half else d - half
        if d < ROPE:
            t[m - d + mate, T_SWAP + m] = 1.0
        for kv in range(KV_HEADS):
            t[kv * HEAD + d, T_DUP + kv * P + m] = 1.0
            if d < ROPE:
                t[kv * HEAD + mate, T_DUPSWAP + kv * P + m] = 1.0
    inv = np.power(np.float32(THETA), -np.arange(0, ROPE, 2, dtype=np.float32) / np.float32(ROPE)).astype(np.float32)
    ang = np.arange(S, dtype=np.float32)[:, None] * inv[None, :]
    cos, sin = np.cos(ang).T, np.sin(ang).T
    t[:, T_COS:T_COS + S] = 1.0
    for m in range(P):
        d = m % HEAD
        if d < ROPE:
            t[m, T_COS:T_COS + S] = cos[d % half]
            t[m, T_SIN:T_SIN + S] = sin[d % half] * (-1.0 if d < half else 1.0)
    return t


class Phase:

    def __init__(self, kind, at, blocks, tiles, kt, first, layer, which, gains, scale, weight):
        self.kind = kind
        self.n_blocks = blocks
        self.tiles = tiles
        self.kt = kt
        self.first = first
        self.layer, self.which = layer, which
        self.gains = gains
        self.scale = scale
        self.weight = weight
        self.block0, self.group0, self.tile0, self.product0, self.ff0, self.norm0, self.hg0 = at


def plan():
    phases = []

    def add(kind, blocks, groups, splits=0, products=0, tiles=0, kt=DT, first=0, layer=0, which=0, gains=(),
            scale=1.0, weight=""):
        at = (0,) * 7 if not phases else ends[-1]
        phases.append(Phase(kind, at, blocks, tiles, kt, first, layer, which, gains, scale, weight))
        normed = 1 if gains else 0
        steps = (blocks, groups, splits, products, tiles, normed, DT * len(gains))
        ends.append(tuple(a + b for a, b in zip(at, steps)))

    ends = []

    def ffn(layer, which, gains):
        for n, (first, tiles) in enumerate(PARTS):
            add("gu", 2 * tiles, 2 * tiles, tiles, tiles, tiles, first=first, layer=layer, which=which)
            last = n == len(PARTS) - 1
            add("final" if last and not gains else "down", DT, DT, kt=tiles, first=first, layer=layer, which=which,
                gains=gains if last else (), scale=0.5)

    add("input", 0, 0, gains=((V_FFN, 0),))
    ffn(0, 0, ((V_MIX, 0),))
    add("xb", DT, DT, DT, DT)
    add("gates", 4, 16, kt=2)
    add("yb", DT, DT, DT, DT)
    add("out", DT, DT, gains=((V_FFN + 8, 0),), weight="lru_w_out")
    ffn(0, 1, ((V_KV, 1), (V_FFN + 16, 0)))
    add("kv", 2, 2)
    ffn(1, 0, ((V_MIX + 8, 0),))
    add("q", DT, DT, 2 * DT)
    add("out", DT, DT, gains=((V_FFN + 24, 0),), weight="attn_w_o")
    ffn(1, 1, ())
    return phases


def trunk_program(nc, x, params, weights, tables, out):
    phases = plan()
    n_blocks = phases[-1].block0 + phases[-1].n_blocks

    with ExitStack() as ctx:
        def sb(name, shape, dt=F32, where=ctx):
            return where.enter_context(nc.sbuf_tensor(name, shape, dt))

        def sem(name):
            return ctx.enter_context(nc.semaphore(name))

        h = sb("h", [P, DT, S])
        hg_hi = sb("hg_hi", [P, DT, S], F32R)
        hg_lo = sb("hg_lo", [P, DT, S], F32R)
        act_hi = sb("act_hi", [P, DT, S], F32R)
        act_lo = sb("act_lo", [P, DT, S], F32R)
        raw = sb("raw", [P, RAW, BLK])
        w_hi = sb("w_hi", [P, RING, BLK], F32R)
        w_lo = sb("w_lo", [P, RING, BLK], F32R)
        rstd = sb("rstd", [P, S])
        sqsum = sb("sqsum", [P, S])
        sq = sb("sq", [P, 2, S])
        tmp = sb("tmp", [P, 4, S])
        tab = sb("tab", [P, T_END])
        vec = sb("vec", [P, P + 8])
        ones_r = sb("ones_r", [P, P], F32R)
        ones = ones_r[:, :].bitcast(F32)
        mask = sb("mask", [P, 2 * P], F32R)
        eps = sb("eps", [P, 1])
        lc = sb("lc", [P, 12, DT])
        stat = sb("stat", [P, 2, 7, 4])

        with ExitStack() as part:
            lru_r = sb("lru_r", [P, DT, S], where=part)
            lru_i = sb("lru_i", [P, DT, S], where=part)
            lru_x = sb("lru_x", [P, DT, S], where=part)
            xpad = sb("xpad", [P, 2, CONV - 1 + S + 1], where=part)
            th = sb("th", [P, 2, S], where=part)
            asq = sb("asq", [P, 2, S], where=part)
        with ExitStack() as part:
            hkv_hi = sb("hkv_hi", [P, DT, S], F32R, where=part)
            hkv_lo = sb("hkv_lo", [P, DT, S], F32R, where=part)
        with ExitStack() as part:
            v_hi = sb("v_hi", [P, 8, KV_HEADS, 2, HEAD], F32R, where=part)
            v_lo = sb("v_lo", [P, 8, KV_HEADS, 2, HEAD], F32R, where=part)
            k_hi = sb("k_hi", [P, KV_HEADS, 2, CHUNK + S], F32R, where=part)
            k_lo = sb("k_lo", [P, KV_HEADS, 2, CHUNK + S], F32R, where=part)
            q_hi = sb("q_hi", [P, 2, 8, 2, CHUNK], F32R, where=part)
            q_lo = sb("q_lo", [P, 2, 8, 2, CHUNK], F32R, where=part)
            with ExitStack() as early:
                k_f32 = sb("k_f32", [P, S], where=early)
                v_pad = sb("v_pad", [P, CHUNK + S], where=early)
            pt_hi = sb("pt_hi", [P, 2, 4, P], F32R, where=part)
            pt_lo = sb("pt_lo", [P, 2, 4, P], F32R, where=part)

        bank = [ctx.enter_context(nc.psum_tensor(f"bank{n}", [P, S], F32)) for n in range(8)]

        prob = sq[:, :, :].rearrange("p b (u k) -> p b u k", u=4)
        sink = vec[:, P:P + 8].rearrange("p (r f) -> p r f", f=2)

        raw_loaded = [sem(f"raw_loaded{n}") for n in range(RAW)]
        x_loaded = [sem(f"x_loaded{t}") for t in range(DT)]
        params_loaded = sem("params_loaded")
        tables_loaded = sem("tables_loaded")
        consts_set = sem("consts_set")
        masks_set = sem("masks_set")
        lru_const = sem("lru_const")
        lru_const_exp = sem("lru_const_exp")
        w_rounded = sem("w_rounded")
        w_ready = sem("w_ready")
        group_done = sem("group_done")
        drained = sem("drained")
        silu_done = sem("silu_done")
        act_product = sem("act_product")
        act_rounded = sem("act_rounded")
        act_split = sem("act_split")
        squared = sem("squared")
        sq_summed = sem("sq_summed")
        hg_rounded = sem("hg_rounded")
        hg_split = sem("hg_split")
        rms_summed = sem("rms_summed")
        rooted = sem("rooted")
        rstd_ready = sem("rstd_ready")
        conv_started = sem("conv_started")
        conv_step = sem("conv_step")
        lru_tanh = sem("lru_tanh")
        lru_decay = sem("lru_decay")
        lru_ix = sem("lru_ix")
        lru_m2 = sem("lru_m2")
        lru_root = sem("lru_root")
        lru_u = sem("lru_u")
        lru_scanned = sem("lru_scanned")
        lru_gelu = sem("lru_gelu")
        kv_pads = sem("kv_pads")
        k_picked = sem("k_picked")
        k_step = sem("k_step")
        k_rounded = sem("k_rounded")
        k_split = sem("k_split")
        v_turned = sem("v_turned")
        v_rounded = sem("v_rounded")
        v_split = sem("v_split")
        q_swapped = sem("q_swapped")
        q_step = sem("q_step")
        q_rounded = sem("q_rounded")
        q_split = sem("q_split")
        scored = sem("scored")
        soft_step = sem("soft_step")
        norm_step = sem("norm_step")
        exped = sem("exped")
        probs_ready = sem("probs_ready")
        p_turned = sem("p_turned")
        p_rounded = sem("p_rounded")
        p_split = sem("p_split")
        pv_done = sem("pv_done")
        out_ready = sem("out_ready")
        stored = sem("stored")

        block = ctx.enter_context(nc.Block())

        def w_view(slot, which, k):
            return which[:, slot, k * P:(k + 1) * P]

        def q_places(ph):
            turned = (bank[6], bank[(ph.group0 + 2) % BANKS])

            def swap_bank(m):
                return bank[(ph.group0 + 3) % BANKS]

            def t_bank(n):
                return turned[n % 2]

            def o_views(n, half, act):
                rows, pair, cp = slice(half * HEAD, (half + 1) * HEAD), n // 4, n % 4
                dst = act[rows, 2 * pair:2 * pair + 2, cp * P:(cp + 1) * P].rearrange("p t (c q) -> p c t q", c=2)
                src = bank[7][rows, :].rearrange("p (c f t q) -> p c f t q", c=2, f=2, t=2)[:, :, half]
                return dst, src
            return t_bank, o_views, swap_bank

        @block.sync
        def _(sp):
            def load(b, n, k_tiles, first=False):
                if not first:
                    sp.wait_ge(w_ready, b - (RAW - 1))
                sp.dma_start(raw[:, n % RAW, 0:k_tiles * P],
                             weights[ds(b, 1), :, 0:k_tiles * P].rearrange("a p c -> (a p) c")
                             ).then_inc(raw_loaded[n % RAW], 16)

            load(0, 0, DT, first=True)
            for t in range(1, DT, 2):
                sp.dma_start(h[:, t, :], x[:, t, :]).then_inc(x_loaded[t], 16)
            for n in range(1, RAW):
                load(n, n, DT, first=True)
            for ph in phases:
                k_tiles = ph.kt if ph.kind in ("down", "final") else DT
                start = RAW if ph.block0 == 0 else 0
                if ph.n_blocks > start:
                    with sp.Fori(0, (ph.n_blocks - start) // RAW) as i:
                        for j in range(RAW):
                            load(ph.block0 + start + RAW * i + j, ph.block0 + start + j, k_tiles)

        @block.gpsimd
        def _(pool):
            nc.gpsimd.memset(ones_r[:, :].bitcast(F32), 1.0).then_inc(consts_set, 1)
            nc.gpsimd.memset(mask[:, :].bitcast(F32), 0.0).then_inc(masks_set, 1)
            pool.wait_ge(masks_set, 1)
            for half in range(2):
                nc.gpsimd.memset(mask[0:1, half * P:half * P + CHUNK].bitcast(F32), MASK).then_inc(masks_set, 1)
            nc.gpsimd.memset(eps[:, :], EPS).then_inc(consts_set, 1)
            kv = next(ph for ph in phases if ph.kind == "kv")
            pool.wait_ge(group_done, kv.group0 + 2)
            pads = 0
            for t in (k_hi, k_lo):
                for zero in (t[:, :, :, 0:CHUNK], t[HEAD:P, :, 0, CHUNK:CHUNK + S], t[0:HEAD, :, 1, CHUNK:CHUNK + S]):
                    if pads:
                        pool.wait_ge(kv_pads, pads)
                    nc.gpsimd.memset(zero.bitcast(F32), 0.0).then_inc(kv_pads, 1)
                    pads += 1

        @block.scalar
        def _(act):
            def round_weights(b, n, group):
                if n + RING >= n_blocks:
                    return
                if group is not None:
                    act.wait_ge(group_done, group + 1)
                act.wait_ge(raw_loaded[n % RAW], (b - n) * (16 // RAW) + 16 * ((n + RING) // RAW + 1))
                slot = (n + RING) % RING
                nc.scalar.activation(w_hi[:, slot, :], raw[:, (n + RING) % RAW, :], ACT.Copy).then_inc(w_rounded, 1)

            def square(ph, o, j):
                act.wait_ge(sq_summed, 9 * ph.norm0 + o)
                nc.scalar.activation(sq[:, j % 2, :], h[:, o, :], ACT.Square).then_inc(squared, 1)

            def gain_head(ph, o):
                for gain, dest in ph.gains:
                    hi = (hkv_hi if dest else hg_hi)
                    nc.scalar.activation(hi[:, o, :], h[:, o, :], ACT.Copy,
                                         scale=vec[:, ds(gain + o, 1)]).then_inc(hg_rounded, 1)

            def root(norm):
                act.wait_ge(rms_summed, norm + 1)
                nc.scalar.activation(rstd[:, :], bank[4][:, :], ACT.Sqrt, bias=eps[:, 0:1],
                                     scale=1.0 / D).then_inc(rooted, 1)

            def decay(t):
                act.wait_ge(lru_tanh, 4 * (t // 2) + t % 2 + 1)
                if t >= 2:
                    act.wait_ge(lru_m2, t - 1)
                nc.scalar.activation(th[:, t % 2, :], lru_r[:, t, :], ACT.Tanh, bias=lc[:, 10, t:t + 1],
                                     scale=lc[:, 10, t:t + 1]).then_inc(lru_decay, 1)
                nc.scalar.activation(lru_r[:, t, :], lru_r[:, t, :], ACT.Exp, bias=lc[:, 11, t:t + 1],
                                     scale=lc[:, 11, t:t + 1]).then_inc(lru_decay, 1)
                act.wait_ge(lru_decay, 3 * t + 2)
                nc.scalar.activation(asq[:, t % 2, :], lru_r[:, t, :], ACT.Square).then_inc(lru_decay, 1)

            def split_k(kv):
                act.wait_ge(k_step, 3 * (kv + 1))
                for half in range(2):
                    rows = slice(half * HEAD, (half + 1) * HEAD)
                    nc.scalar.activation(k_hi[rows, kv, half, CHUNK:CHUNK + S], sq[rows, 1, :],
                                         ACT.Copy).then_inc(k_rounded, 1)

            def split_v(n):
                act.wait_ge(v_turned, n + 1)
                for dup in range(2):
                    nc.scalar.activation(v_hi[:, 4 * n:4 * n + 4, :, dup, :].rearrange("p c v d -> p (c v) d"),
                                         bank[4 + n][:, :].rearrange("p (c d) -> p c d", d=HEAD),
                                         ACT.Copy).then_inc(v_rounded, 1)

            act.dma_start(vec[:, :], params).then_inc(params_loaded, 16)
            for t in range(0, DT, 2):
                act.dma_start(h[:, t, :], x[:, t, :]).then_inc(x_loaded[t], 16)
            act.dma_start(tab[:, :], tables).then_inc(tables_loaded, 16)

            for idx, ph in enumerate(phases):
                b0, g0 = ph.block0, ph.group0
                if ph.kind == "input":
                    round_weights(-RING, -RING, None)
                    act.wait_ge(params_loaded, 16)
                    for o in range(DT):
                        act.wait_ge(x_loaded[o], 16)
                        gain_head(ph, o)
                    round_weights(1 - RING, 1 - RING, None)
                    for o in range(DT):
                        square(ph, o, o)
                        if o in (3, 7):
                            round_weights(2 + o // 4 - RING, 2 + o // 4 - RING, None)
                    act.wait_ge(consts_set, 2)
                    root(ph.norm0)
                elif ph.kind == "gu":
                    def ffn_tiles(i, after=()):
                        for j in range(4):
                            if j % 2 == 0:
                                act.wait_ge(drained, g0 + 4 * i + j + 1)
                                nc.scalar.activation(tmp[:, 1, :], tmp[:, 0, :], ACT.Silu).then_inc(silu_done, 1)
                            round_weights(b0 + 4 * i + j, b0 + j, g0 + 4 * i + j)
                            if j % 2 == 1:
                                act.wait_ge(act_product, ph.product0 + 2 * i + j // 2 + 1)
                                nc.scalar.activation(act_hi[:, 2 * i + j // 2, :], tmp[:, 3, :],
                                                     ACT.Copy).then_inc(act_rounded, 1)
                            if j < len(after):
                                after[j]()
                    def decay_exp():
                        act.wait_ge(lru_const, 2)
                        nc.scalar.activation(lc[:, 2, :], lc[:, 1, :], ACT.Exp, scale=-1.0).then_inc(lru_const_exp, 1)

                    start = 0
                    if phases[idx - 1].kind == "input":
                        ffn_tiles(0, (decay_exp,))
                        start = 1
                    if phases[idx - 1].kind == "kv":
                        ffn_tiles(0, (lambda: (split_k(0), split_k(1)), lambda: (split_v(0), split_v(1))))
                        start = 1
                    with act.Fori(start, ph.tiles // 2) as i:
                        ffn_tiles(i)
                elif ph.kind == "down" or ph.kind == "out":
                    with act.Fori(0, DT // 4) as i:
                        for j in range(4):
                            o = 4 * i + j
                            if ph.gains:
                                act.wait_ge(drained, g0 + o + 1)
                                square(ph, o, j)
                            round_weights(b0 + o, b0 + j, g0 + o)
                            gain_head(ph, o)
                    if ph.gains:
                        root(ph.norm0)
                elif ph.kind == "xb":
                    with act.Fori(0, DT // 4) as i:
                        for j in range(4):
                            t = 4 * i + j
                            round_weights(b0 + t, b0 + j, g0 + t)
                            act.wait_ge(drained, g0 + t + 1)
                            nc.scalar.activation(lru_x[:, t, :], xpad[:, j % 2, 0:S], ACT.Identity,
                                                 bias=vec[:, ds(V_CONVB + t, 1)],
                                                 scale=vec[:, ds(V_CONVW + t, 1)]).then_inc(conv_started, 1)
                            act.wait_ge(act_product, ph.product0 + t + 1)
                            nc.scalar.activation(act_hi[:, t, :], lru_x[:, t, :], ACT.Copy).then_inc(act_rounded, 1)
                elif ph.kind == "gates":
                    for hb in range(4):
                        for n in range(4):
                            g, t = n // 2, 2 * hb + n % 2
                            act.wait_ge(drained, g0 + 4 * hb + n + 1)
                            z = (lru_i if g else lru_r)[:, t, :]
                            nc.scalar.activation(z, z, ACT.Tanh, scale=0.5).then_inc(lru_tanh, 1)
                        round_weights(b0 + hb, b0 + hb, g0 + 4 * hb + 3)
                        if hb == 1:
                            act.wait_ge(lru_const, LRU_CONST_STEPS)
                        if hb:
                            decay(hb - 1)
                elif ph.kind == "yb":
                    def root_m2(t):
                        act.wait_ge(lru_m2, t + 1)
                        nc.scalar.activation(tmp[:, t % 4, :], tmp[:, t % 4, :], ACT.Sqrt).then_inc(lru_root, 1)

                    def gelu(t):
                        act.wait_ge(drained, g0 + t + 1)
                        nc.scalar.activation(lru_x[:, t, :], lru_x[:, t, :], ACT.Gelu_apprx_tanh).then_inc(lru_gelu, 1)

                    def head_of_y(t):
                        act.wait_ge(act_product, ph.product0 + t + 1)
                        nc.scalar.activation(act_hi[:, t, :], tmp[:, t % 4, :], ACT.Copy).then_inc(act_rounded, 1)

                    beside = ([(decay, 3)], [(root_m2, t) for t in range(4)], [(decay, 4), (decay, 5)],
                              [(decay, 6), (decay, 7)], [(root_m2, t) for t in range(4, 8)],
                              [(gelu, t) for t in range(5)], [(gelu, 5), (head_of_y, 0), (head_of_y, 1)],
                              [(gelu, 6), (head_of_y, 2), (head_of_y, 3), (gelu, 7), (head_of_y, 4), (head_of_y, 5),
                               (head_of_y, 6), (head_of_y, 7)])
                    for s in range(DT):
                        round_weights(b0 + s, b0 + s, g0 + s)
                        for what, t in beside[s]:
                            what(t)
                elif ph.kind == "kv":
                    for j in range(2):
                        round_weights(b0 + j, b0 + j, g0 + j)
                elif ph.kind == "q":
                    def head_of_q(m):
                        act.wait_ge(q_step, 3 * (m + 1))
                        nc.scalar.activation(q_hi[:, (m // 2) % 2, :, m % 2, :],
                                             tmp[:, 2, :].rearrange("p (c q) -> p c q", q=CHUNK),
                                             ACT.Copy).then_inc(q_rounded, 1)

                    def exps(n):
                        par = n % 2
                        act.wait_ge(soft_step, 4 * (n + 1))
                        for u in range(4):
                            nc.scalar.activation(prob[:, par, u, :], bank[4 + par][:, u * P:(u + 1) * P], ACT.Exp,
                                                 bias=stat[:, par, 1, u:u + 1], scale=HEAD ** -0.5,
                                                 accum_out=stat[:, par, 4, u:u + 1])
                        nc.scalar.activation(stat[:, par, 3, :], stat[:, par, 2, :], ACT.Exp).then_inc(exped, 1)

                    def head_of_p(n):
                        act.wait_ge(p_turned, n + 1)
                        nc.scalar.activation(pt_hi[:, n % 2, :, :].rearrange("p u q -> p (u q)"), t_bank(n)[:, :],
                                             ACT.Copy).then_inc(p_rounded, 1)

                    def head_of_o(n):
                        act.wait_ge(pv_done, n + 1)
                        for half in range(2):
                            dst, src = o_views(n, half, act_hi)
                            ins = nc.scalar.activation(dst, src, ACT.Copy)
                        ins.then_inc(act_rounded, 1)

                    t_bank, o_views, swap_bank = q_places(ph)
                    def round_q(m):
                        if m < DT:
                            round_weights(b0 + m, b0 + m, g0 + m)

                    for m in range(2):
                        round_q(m)
                    for m in range(2):
                        head_of_q(m)
                    round_q(2)
                    for pair in range(4):
                        n, m = 4 * pair, 2 * pair + 2
                        exps(n)
                        exps(n + 1)
                        head_of_p(n)
                        if m < DT:
                            head_of_q(m)
                        round_q(m + 1)
                        head_of_p(n + 1)
                        exps(n + 2)
                        head_of_o(n)
                        exps(n + 3)
                        head_of_o(n + 1)
                        if m < DT:
                            head_of_q(m + 1)
                        head_of_p(n + 2)
                        round_q(m + 2)
                        head_of_p(n + 3)
                        head_of_o(n + 2)
                        head_of_o(n + 3)
                elif ph.kind == "final":
                    for o in range(DT):
                        act.wait_ge(drained, g0 + o + 1)
                        square(ph, o, o)
                        round_weights(b0 + o, b0 + o, g0 + o)
                    root(ph.norm0)
                    for t in range(DT):
                        act.wait_ge(out_ready, t + 1)
                        act.dma_start(out[:, t, :], h[:, t, :]).then_inc(stored, 16)
                    act.wait_ge(stored, 16 * DT)

        @block.vector
        def _(dve):
            def split_weights(b, n):
                if n + RING >= n_blocks:
                    return
                dve.wait_ge(w_rounded, b + RING + 1)
                slot = (n + RING) % RING
                nc.vector.tensor_tensor(w_lo[:, slot, :], raw[:, (n + RING) % RAW, :],
                                        w_hi[:, slot, :].bitcast(F32), ALU.subtract).then_inc(w_ready, 1)

            def residual_open(ph):
                nc.vector.memset(sqsum[:, :], 0.0).then_inc(sq_summed, 1)

            def add_square(ph, o, j):
                dve.wait_ge(squared, DT * ph.norm0 + o + 1)
                dve.wait_ge(sq_summed, 9 * ph.norm0 + o + 1)
                nc.vector.tensor_tensor(sqsum[:, :], sqsum[:, :], sq[:, j % 2, :], ALU.add).then_inc(sq_summed, 1)

            def gain_rest(ph, o):
                for n, (gain, dest) in enumerate(ph.gains):
                    hi, lo = (hkv_hi, hkv_lo) if dest else (hg_hi, hg_lo)
                    dve.wait_ge(hg_rounded, ph.hg0 + len(ph.gains) * o + n + 1)
                    nc.vector.scalar_tensor_tensor(lo[:, o, :], h[:, o, :], vec[:, ds(gain + o, 1)],
                                                   hi[:, o, :].bitcast(F32), ALU.mult,
                                                   ALU.subtract).then_inc(hg_split, 1)

            def invert(norm):
                dve.wait_ge(rooted, norm + 1)
                nc.vector.reciprocal(rstd[:, :], rstd[:, :]).then_inc(rstd_ready, 1)
                dve.wait_ge(rstd_ready, norm + 1)

            def drain_scaled(dst, g, n):
                dve.wait_ge(group_done, g + 1)
                nc.vector.tensor_tensor(dst, bank[n % BANKS][:, :], rstd[:, :], ALU.mult).then_inc(drained, 1)

            def rest(t, src, count):
                dve.wait_ge(act_rounded, count + 1)
                nc.vector.tensor_tensor(act_lo[:, t, :], src, act_hi[:, t, :].bitcast(F32),
                                        ALU.subtract).then_inc(act_split, 1)

            def gated_input(t):
                dve.wait_ge(lru_tanh, 4 * (t // 2) + 2 + t % 2 + 1)
                nc.vector.scalar_tensor_tensor(lru_i[:, t, :], lru_i[:, t, :], 1.0, lru_x[:, t, :], ALU.add,
                                               ALU.mult).then_inc(lru_ix, 1)

            def decay_rest(t):
                dve.wait_ge(lru_decay, 3 * (t + 1))
                if t >= 4:
                    dve.wait_ge(lru_u, t - 3)
                nc.vector.scalar_tensor_tensor(tmp[:, t % 4, :], asq[:, t % 2, :], 1.0, th[:, t % 2, :], ALU.add,
                                               ALU.mult).then_inc(lru_m2, 1)

            lc_steps = [0]

            def lc_op(ins):
                lc_steps[0] += 1
                ins.then_inc(lru_const, 1)
                dve.wait_ge(lru_const, lc_steps[0])

            def lru_constants():
                a = vec[:, V_A:V_A + DT]
                c = lambda n: lc[:, n, :]
                lc_op(nc.vector.tensor_scalar(c(0), a, -1.0, None, ALU.mult))
                lc_op(nc.vector.tensor_tensor(c(1), a, c(0), ALU.max))
                dve.wait_ge(lru_const_exp, 1)
                lc_op(nc.vector.tensor_scalar(c(3), c(2), 2.0, None, ALU.add))
                lc_op(nc.vector.reciprocal(c(4), c(3)))
                lc_op(nc.vector.tensor_tensor(c(5), c(2), c(4), ALU.mult))
                lc_op(nc.vector.tensor_tensor(c(6), c(5), c(5), ALU.mult))
                lc_op(nc.vector.tensor_scalar(c(7), c(6), 1.0 / 15, 1.0 / 13, ALU.mult, ALU.add))
                for k in (11, 9, 7, 5, 3, 1):
                    lc_op(nc.vector.tensor_tensor(c(7), c(7), c(6), ALU.mult))
                    lc_op(nc.vector.tensor_scalar(c(7), c(7), 1.0 / k, None, ALU.add))
                lc_op(nc.vector.tensor_tensor(c(7), c(7), c(5), ALU.mult))
                lc_op(nc.vector.tensor_scalar(c(8), c(0), 0.0, None, ALU.max))
                lc_op(nc.vector.scalar_tensor_tensor(c(9), c(7), 2.0, c(8), ALU.mult, ALU.add))
                lc_op(nc.vector.tensor_scalar(c(10), c(9), 4.0, None, ALU.mult))
                lc_op(nc.vector.tensor_scalar(c(11), c(9), -4.0, None, ALU.mult))
                assert lc_steps[0] == LRU_CONST_STEPS

            def rotate_k(kv):
                dve.wait_ge(k_picked, kv + 1)
                if kv:
                    dve.wait_ge(k_split, 1)
                nc.vector.tensor_tensor(sq[:, 0, :], bank[4 + 2 * kv][:, :], tab[:, T_COS:T_COS + S],
                                        ALU.mult).then_inc(k_step, 1)
                nc.vector.tensor_tensor(sq[:, 1, :], bank[5 + 2 * kv][:, :], tab[:, T_SIN:T_SIN + S],
                                        ALU.mult).then_inc(k_step, 1)
                dve.wait_ge(k_step, 3 * kv + 2)
                nc.vector.tensor_tensor(sq[:, 1, :], sq[:, 1, :], sq[:, 0, :], ALU.add).then_inc(k_step, 1)
                dve.wait_ge(k_rounded, 2 * kv + 2)
                for half in range(2):
                    rows = slice(half * HEAD, (half + 1) * HEAD)
                    ins = nc.vector.tensor_tensor(k_lo[rows, kv, half, CHUNK:CHUNK + S], sq[rows, 1, :],
                                                  k_hi[rows, kv, half, CHUNK:CHUNK + S].bitcast(F32), ALU.subtract)
                ins.then_inc(k_split, 1)

            def rest_of_v(n):
                dve.wait_ge(v_rounded, 2 * n + 2)
                for dup in range(2):
                    at = (slice(None), slice(4 * n, 4 * n + 4), slice(None), dup, slice(None))
                    ins = nc.vector.tensor_tensor(v_lo[at].rearrange("p c v d -> p (c v) d"),
                                                  bank[4 + n][:, :].rearrange("p (c d) -> p c d", d=HEAD),
                                                  v_hi[at].rearrange("p c v d -> p (c v) d").bitcast(F32),
                                                  ALU.subtract)
                ins.then_inc(v_split, 1)

            for idx, ph in enumerate(phases):
                b0, g0 = ph.block0, ph.group0
                if ph.kind == "input":
                    residual_open(ph)
                    dve.wait_ge(params_loaded, 16)
                    split_weights(-RING, -RING)
                    for o in range(DT):
                        gain_rest(ph, o)
                    split_weights(1 - RING, 1 - RING)
                    for o in range(DT):
                        add_square(ph, o, o)
                        if o in (3, 7):
                            split_weights(2 + o // 4 - RING, 2 + o // 4 - RING)
                    invert(ph.norm0)
                elif ph.kind == "gu":
                    def ffn_tiles(i, after=()):
                        for j in range(4):
                            t = 2 * i + j // 2
                            drain_scaled(tmp[:, 2 if j % 2 else 0, :], g0 + 4 * i + j, g0 + j)
                            if j % 2:
                                dve.wait_ge(silu_done, ph.ff0 + t + 1)
                                dve.wait_ge(drained, g0 + 4 * i + j + 1)
                                nc.vector.tensor_tensor(tmp[:, 3, :], tmp[:, 1, :], tmp[:, 2, :],
                                                        ALU.mult).then_inc(act_product, 1)
                            split_weights(b0 + 4 * i + j, b0 + j)
                            if j % 2:
                                rest(t, tmp[:, 3, :], ph.tile0 + t)
                            if j < len(after):
                                after[j]()
                    start = 0
                    if phases[idx - 1].kind in ("input", "kv"):
                        start = 1
                        ffn_tiles(0, (lambda: (rotate_k(0), rotate_k(1)), lambda: (rest_of_v(0), rest_of_v(1)))
                                  if phases[idx - 1].kind == "kv" else (lru_constants,))
                    with dve.Fori(start, ph.tiles // 2) as i:
                        ffn_tiles(i)
                elif ph.kind in ("down", "out"):
                    if ph.gains:
                        residual_open(ph)
                    with dve.Fori(0, DT // 4) as i:
                        for j in range(4):
                            o = 4 * i + j
                            dve.wait_ge(group_done, g0 + o + 1)
                            nc.vector.scalar_tensor_tensor(h[:, o, :], bank[(g0 + j) % BANKS][:, :], ph.scale,
                                                           h[:, o, :], ALU.mult, ALU.add).then_inc(drained, 1)
                            if ph.gains:
                                add_square(ph, o, j)
                            split_weights(b0 + o, b0 + j)
                            gain_rest(ph, o)
                    if ph.gains:
                        invert(ph.norm0)
                elif ph.kind == "xb":
                    nc.vector.memset(xpad[:, :, 0:CONV - 1], 0.0)

                    def tap(i, j, k):
                        t = 4 * i + j
                        if k > 1:
                            dve.wait_ge(conv_step, 2 * t + k - 1)
                        else:
                            dve.wait_ge(conv_started, t + 1)
                        nc.vector.scalar_tensor_tensor(
                            lru_x[:, t, :], xpad[:, j % 2, k:k + S], vec[:, ds(V_CONVW + 8 * k + t, 1)],
                            lru_x[:, t, :], ALU.mult, ALU.add).then_inc(conv_step if k < CONV - 1 else act_product, 1)

                    def xb_tiles(i, first):
                        for j in range(4):
                            t = 4 * i + j
                            drain_scaled(xpad[:, j % 2, CONV - 1:CONV - 1 + S], g0 + t, g0 + j)
                            split_weights(b0 + t, b0 + j)
                            tap(i, j, 1)
                            if not (first and j == 0):
                                rest(t - 1, lru_x[:, t - 1, :], ph.tile0 + t - 1)
                            tap(i, j, 2)
                            tap(i, j, 3)
                    xb_tiles(0, True)
                    with dve.Fori(1, DT // 4) as i:
                        xb_tiles(i, False)
                    rest(DT - 1, lru_x[:, DT - 1, :], ph.tile0 + DT - 1)
                elif ph.kind == "gates":
                    for hb in range(4):
                        for n in range(4):
                            g, t = n // 2, 2 * hb + n % 2
                            dve.wait_ge(group_done, g0 + 4 * hb + n + 1)
                            col = V_GATEB + 8 * g + t
                            nc.vector.tensor_scalar((lru_i if g else lru_r)[:, t, :], bank[(g0 + n) % BANKS][:, :],
                                                    vec[:, col:col + 1], None, ALU.add).then_inc(drained, 1)
                        if hb:
                            split_weights(b0 + hb - 1, b0 + hb - 1)
                            gated_input(2 * hb - 2)
                            gated_input(2 * hb - 1)
                        if hb >= 2:
                            decay_rest(hb - 2)
                    split_weights(b0 + 3, b0 + 3)
                elif ph.kind == "yb":
                    def scan(t):
                        dve.wait_ge(lru_root, t + 1)
                        dve.wait_ge(lru_ix, t + 1)
                        nc.vector.scalar_tensor_tensor(lru_i[:, t, :], tmp[:, t % 4, :], 0.5, lru_i[:, t, :],
                                                       ALU.mult, ALU.mult).then_inc(lru_u, 1)
                        dve.wait_ge(lru_u, t + 1)
                        nc.vector.tensor_tensor_scan(lru_r[:, t, :], lru_r[:, t, :], lru_i[:, t, :], 0.0,
                                                     ALU.mult, ALU.add).then_inc(lru_scanned, 1)

                    def product(t):
                        dve.wait_ge(lru_gelu, t + 1)
                        dve.wait_ge(lru_scanned, t + 1)
                        if t >= 4:
                            dve.wait_ge(act_split, ph.tile0 + t - 3)
                        nc.vector.tensor_tensor(tmp[:, t % 4, :], lru_r[:, t, :], lru_x[:, t, :],
                                                ALU.mult).then_inc(act_product, 1)

                    def rest_of_y(t):
                        rest(t, tmp[:, t % 4, :], ph.tile0 + t)

                    beside = ([(gated_input, 6), (gated_input, 7), (decay_rest, 2), (decay_rest, 3)],
                              [(scan, 0), (scan, 1)], [(scan, 2), (scan, 3), (decay_rest, 4), (decay_rest, 5)],
                              [(decay_rest, 6), (decay_rest, 7)], [(scan, 4), (scan, 5)], [(scan, 6), (scan, 7)],
                              [(product, 0), (product, 1), (rest_of_y, 0), (rest_of_y, 1)],
                              [(product, 2), (product, 3), (rest_of_y, 2), (product, 4), (rest_of_y, 3), (product, 5),
                               (rest_of_y, 4), (product, 6), (rest_of_y, 5), (product, 7), (rest_of_y, 6),
                               (rest_of_y, 7)])
                    for s in range(DT):
                        drain_scaled(lru_x[:, s, :], g0 + s, g0 + s)
                        split_weights(b0 + s, b0 + s)
                        for what, t in beside[s]:
                            what(t)
                elif ph.kind == "kv":
                    nc.vector.memset(v_pad[:, 0:CHUNK], 0.0)
                    drain_scaled(k_f32[:, :], g0, g0)
                    split_weights(b0, b0)
                    drain_scaled(v_pad[:, CHUNK:CHUNK + S], g0 + 1, g0 + 1)
                    split_weights(b0 + 1, b0 + 1)
                elif ph.kind == "q":
                    t_bank, o_views, swap_bank = q_places(ph)

                    def drain_q(m):
                        if m >= 2:
                            dve.wait_ge(q_split, m - 1)
                        dve.wait_ge(group_done, g0 + m + 1)
                        nc.vector.tensor_tensor(tmp[:, m % 2, :], bank[(g0 + m % 2) % BANKS][:, :], rstd[:, :],
                                                ALU.mult).then_inc(drained, 1)

                    def split_q(m):
                        split_weights(b0 + m, b0 + m)

                    def cos_q(m):
                        dve.wait_ge(drained, g0 + m + 1)
                        if m:
                            dve.wait_ge(q_split, m)
                        nc.vector.tensor_tensor(tmp[:, 2, :], tmp[:, m % 2, :], tab[:, T_COS:T_COS + S],
                                                ALU.mult).then_inc(q_step, 1)

                    def sin_q(m):
                        dve.wait_ge(q_swapped, m + 1)
                        nc.vector.tensor_tensor(tmp[:, 3, :], swap_bank(m)[:, :], tab[:, T_SIN:T_SIN + S],
                                                ALU.mult).then_inc(q_step, 1)
                        dve.wait_ge(q_step, 3 * m + 2)
                        nc.vector.tensor_tensor(tmp[:, 2, :], tmp[:, 2, :], tmp[:, 3, :],
                                                ALU.add).then_inc(q_step, 1)
                        dve.wait_ge(q_rounded, m + 1)
                        nc.vector.tensor_tensor(q_lo[:, (m // 2) % 2, :, m % 2, :],
                                                tmp[:, 2, :].rearrange("p (c q) -> p c q", q=CHUNK),
                                                q_hi[:, (m // 2) % 2, :, m % 2, :].bitcast(F32),
                                                ALU.subtract).then_inc(q_split, 1)

                    def maxima(n):
                        par, pair = n % 2, n // 4
                        dve.wait_ge(scored, n + 1)
                        mx, neg, arg = (stat[:, par, r, :] for r in range(3))
                        two = lambda ap: ap.rearrange("p (c f) -> p c f", f=2)
                        sinks = sink[:, pair, :].unsqueeze(1).broadcast_to([P, 2, 2])
                        nc.vector.tensor_reduce(mx, bank[4 + par][:, :].rearrange("p (u k) -> p u k", u=4), AX_X,
                                                ALU.max).then_inc(soft_step, 1)
                        dve.wait_ge(soft_step, 4 * n + 1)
                        nc.vector.scalar_tensor_tensor(two(mx), two(mx), HEAD ** -0.5, sinks, ALU.mult,
                                                       ALU.max).then_inc(soft_step, 1)
                        dve.wait_ge(soft_step, 4 * n + 2)
                        nc.vector.tensor_scalar(neg, mx, -1.0, None, ALU.mult).then_inc(soft_step, 1)
                        nc.vector.tensor_tensor(two(arg), sinks, two(mx), ALU.subtract).then_inc(soft_step, 1)

                    def normalise(n):
                        par = n % 2
                        dve.wait_ge(exped, n + 1)
                        es, sums, den, inv = (stat[:, par, r, :] for r in range(3, 7))
                        nc.vector.tensor_tensor(den, sums, es, ALU.add).then_inc(norm_step, 1)
                        dve.wait_ge(norm_step, 2 * n + 1)
                        nc.vector.reciprocal(inv, den).then_inc(norm_step, 1)
                        dve.wait_ge(norm_step, 2 * n + 2)
                        nc.vector.tensor_tensor(prob[:, par, :, :], prob[:, par, :, :],
                                                inv.unsqueeze(2).broadcast_to([P, 4, P]),
                                                ALU.mult).then_inc(probs_ready, 1)

                    def rest_of_p(n):
                        dve.wait_ge(p_rounded, n + 1)
                        nc.vector.tensor_tensor(pt_lo[:, n % 2, :, :].rearrange("p u q -> p (u q)"), t_bank(n)[:, :],
                                                pt_hi[:, n % 2, :, :].rearrange("p u q -> p (u q)").bitcast(F32),
                                                ALU.subtract).then_inc(p_split, 1)

                    def rest_of_o(n):
                        dve.wait_ge(act_rounded, ph.tile0 + n + 1)
                        for half in range(2):
                            dst, src = o_views(n, half, act_lo)
                            hi, _ = o_views(n, half, act_hi)
                            ins = nc.vector.tensor_tensor(dst, src, hi.bitcast(F32), ALU.subtract)
                        ins.then_inc(act_split, 1)

                    for m in range(2):
                        drain_q(m)
                        split_q(m)
                    for m in range(2):
                        cos_q(m)
                        sin_q(m)
                    drain_q(2)
                    split_q(2)
                    for pair in range(4):
                        n, m = 4 * pair, 2 * pair + 2
                        maxima(n)
                        maxima(n + 1)
                        normalise(n)
                        normalise(n + 1)
                        if m < DT:
                            cos_q(m)
                            drain_q(m + 1)
                        rest_of_p(n)
                        if m < DT:
                            sin_q(m)
                        maxima(n + 2)
                        rest_of_p(n + 1)
                        if m < DT:
                            split_q(m + 1)
                        normalise(n + 2)
                        rest_of_o(n)
                        maxima(n + 3)
                        if m < DT:
                            cos_q(m + 1)
                        rest_of_o(n + 1)
                        if m < DT:
                            sin_q(m + 1)
                        normalise(n + 3)
                        if m + 2 < DT:
                            drain_q(m + 2)
                        rest_of_p(n + 2)
                        if m + 2 < DT:
                            split_q(m + 2)
                        rest_of_p(n + 3)
                        rest_of_o(n + 2)
                        rest_of_o(n + 3)
                elif ph.kind == "final":
                    residual_open(ph)
                    for o in range(DT):
                        dve.wait_ge(group_done, g0 + o + 1)
                        nc.vector.scalar_tensor_tensor(h[:, o, :], bank[(g0 + o) % BANKS][:, :], ph.scale,
                                                       h[:, o, :], ALU.mult, ALU.add).then_inc(drained, 1)
                        add_square(ph, o, o)
                        split_weights(b0 + o, b0 + o)
                    invert(ph.norm0)
                    for t in range(DT):
                        nc.vector.scalar_tensor_tensor(h[:, t, :], h[:, t, :], vec[:, V_FINAL + t:V_FINAL + t + 1],
                                                       rstd[:, :], ALU.mult, ALU.mult).then_inc(out_ready, 1)

        @block.tensor
        def _(pe):
            def group(b, n_slot, g, n_bank, k_tiles, x_hi, x_lo, w_tile, ready=None, wait_block=True):
                if wait_block:
                    pe.wait_ge(w_ready, b + 1)
                if n_bank >= BANKS:
                    pe.wait_ge(drained, g + 1 - BANKS)
                dst = bank[n_bank % BANKS][:, :]
                slot = n_slot % RING
                for k in range(k_tiles):
                    if ready is not None:
                        ready(k)
                    nc.tensor.matmul(dst, w_tile(w_hi, slot, k), x_hi[:, k, :], start=(k == 0), stop=False)
                    nc.tensor.matmul(dst, w_tile(w_hi, slot, k), x_lo[:, k, :], start=False, stop=False)
                    mm = nc.tensor.matmul(dst, w_tile(w_lo, slot, k), x_hi[:, k, :], start=False,
                                          stop=(k == k_tiles - 1))
                mm.then_inc(group_done, 1)

            def tile(w, slot, k):
                return w[:, slot, k * P:(k + 1) * P]

            def sum_squares(norm):
                pe.wait_ge(sq_summed, 9 * (norm + 1))
                nc.tensor.matmul(bank[4][:, :], ones, sqsum[:, :], start=True, stop=True).then_inc(rms_summed, 1)

            ident = tab[:, T_ID:T_ID + P]
            pending = []

            def run(ph, n, one):
                start = 0
                if pending:
                    for j in range(4):
                        one(0, j)
                        what = pending.pop(0) if pending else None
                        if what is not None:
                            what()
                    start = 1
                if n // 4 > start:
                    with pe.Fori(start, n // 4) as i:
                        for j in range(4):
                            one(i, j)

            for idx, ph in enumerate(phases):
                b0, g0 = ph.block0, ph.group0
                ph_gains = next((len(q.gains) for q in reversed(phases[:idx]) if q.gains), 1)

                def hg_ready(k):
                    pe.wait_ge(hg_split, ph.hg0 - DT * ph_gains + (k + 1) * ph_gains)

                if ph.kind == "input":
                    pe.wait_ge(consts_set, 2)
                    pending += [None, lambda n=ph.norm0: sum_squares(n)]
                elif ph.kind in ("gu", "xb", "yb"):
                    def one(i, j):
                        group(b0 + 4 * i + j, b0 + j, g0 + 4 * i + j, g0 + j, DT, hg_hi, hg_lo, tile,
                              ready=hg_ready if j == 0 else None)
                    run(ph, ph.n_blocks, one)
                elif ph.kind in ("down", "out"):
                    def split_ready(k):
                        pe.wait_ge(act_split, ph.tile0 - ph.kt + k + 1)
                    if ph.kind == "out" and ph.weight == "attn_w_o":
                        def split_ready(k):
                            pe.wait_ge(act_split, ph.tile0 - 2 * DT + 4 * (k // 2) + 4)

                    def one(i, j):
                        group(b0 + 4 * i + j, b0 + j, g0 + 4 * i + j, g0 + j, ph.kt, act_hi, act_lo, tile,
                              ready=split_ready if j == 0 else None)
                    run(ph, DT, one)
                    if ph.gains:
                        if phases[idx + 1].kind == "gu":
                            pending.append(None)
                        pending.append(lambda n=ph.norm0: sum_squares(n))
                elif ph.kind == "gates":
                    xb = phases[idx - 1]
                    for hb in range(4):
                        for n in range(4):
                            g, ot = n // 2, n % 2

                            def gate_tile(w, slot, k):
                                at = g * 512 + k * 256 + ot * P
                                return w[:, slot, at:at + P]

                            def xc_ready(k):
                                pe.wait_ge(act_split, xb.tile0 + 2 * hb + k + 1)
                            group(b0 + hb, b0 + hb, g0 + 4 * hb + n, g0 + n, 2, act_hi[:, 2 * hb:2 * hb + 2, :],
                                  act_lo[:, 2 * hb:2 * hb + 2, :], gate_tile, ready=xc_ready, wait_block=(n == 0))
                elif ph.kind == "kv":
                    for j in range(2):
                        group(b0 + j, b0 + j, g0 + j, g0 + j, DT, hkv_hi, hkv_lo, tile, ready=hg_ready)
                        if j == 0:
                            pending.pop(0)()

                    def pick_k(g=g0):
                        pe.wait_ge(tables_loaded, 16)
                        pe.wait_ge(drained, g + 1)
                        for kv in range(KV_HEADS):
                            nc.tensor.matmul(bank[4 + 2 * kv][:, :], tab[:, T_DUP + kv * P:T_DUP + (kv + 1) * P],
                                             k_f32[:, :], start=True, stop=True)
                            nc.tensor.matmul(bank[5 + 2 * kv][:, :],
                                             tab[:, T_DUPSWAP + kv * P:T_DUPSWAP + (kv + 1) * P], k_f32[:, :], start=True,
                                             stop=True).then_inc(k_picked, 1)

                    def turn_v(g=g0):
                        pe.wait_ge(drained, g + 2)
                        pe.wait_ge(k_step, 2)
                        for n in range(2):
                            for c in range(4):
                                t0 = (4 * n + c) * CHUNK
                                mm = nc.tensor.transpose(bank[4 + n][:, c * P:(c + 1) * P], v_pad[:, t0:t0 + P],
                                                         ident)
                            mm.then_inc(v_turned, 1)
                    pending += [pick_k, turn_v]
                elif ph.kind == "q":
                    t_bank, o_views, swap_bank = q_places(ph)

                    def project_q(m):
                        pe.wait_ge(drained, g0 + max(m - 1, 0))
                        group(b0 + m, b0 + m, g0 + m, g0 + m % 2, DT, hg_hi, hg_lo, tile,
                              ready=hg_ready if m == 0 else None)

                    def swap_q(m):
                        pe.wait_ge(drained, g0 + m + 1)
                        if m:
                            pe.wait_ge(q_step, 3 * m)
                        nc.tensor.matmul(swap_bank(m)[:, :], tab[:, T_SWAP:T_SWAP + P], tmp[:, m % 2, :],
                                         start=True, stop=True).then_inc(q_swapped, 1)

                    def score(n):
                        pair, cp = n // 4, n % 4
                        pe.wait_ge(q_split, 2 * pair + 2)
                        if n >= 2:
                            pe.wait_ge(exped, n - 1)
                        for u in range(2):
                            c = 2 * cp + u
                            dst = bank[4 + n % 2][:, 2 * u * P:2 * (u + 1) * P]
                            if c == 0:
                                nc.tensor.matmul(dst, ones_r[:, :], mask[:, :], start=True, stop=False)
                            for step, (q, k) in enumerate(((q_hi, k_hi), (q_hi, k_lo), (q_lo, k_hi))):
                                mm = nc.tensor.matmul(dst, q[:, pair % 2, c, :, :].rearrange("p t q -> p (t q)"),
                                                      k[:, pair // 2, :, c * CHUNK:c * CHUNK + P],
                                                      start=(step == 0 and c > 0), stop=(step == 2))
                        mm.then_inc(scored, 1)

                    def turn_p(n):
                        pe.wait_ge(probs_ready, n + 1)
                        if n >= 2:
                            pe.wait_ge(p_split, n - 1)
                        for u in range(4):
                            mm = nc.tensor.transpose(t_bank(n)[:, u * P:(u + 1) * P], prob[:, n % 2, u, :], ident)
                        mm.then_inc(p_turned, 1)

                    def weigh_v(n):
                        pair, cp = n // 4, n % 4
                        pe.wait_ge(p_split, n + 1)
                        if n:
                            pe.wait_ge(act_split, ph.tile0 + n)
                        for u in range(2):
                            dst = bank[7][:, 2 * u * P:2 * (u + 1) * P]
                            for step, (v, p) in enumerate(((v_hi, pt_hi), (v_hi, pt_lo), (v_lo, pt_hi))):
                                mm = nc.tensor.matmul(
                                    dst, v[:, 2 * cp + u, pair // 2, :, :].rearrange("p a d -> p (a d)"),
                                    p[:, n % 2, 2 * u:2 * u + 2, :], start=(step == 0), stop=(step == 2))
                        mm.then_inc(pv_done, 1)

                    project_q(0)
                    pending.pop(0)()
                    project_q(1)
                    project_q(2)
                    pe.wait_ge(k_split, KV_HEADS)
                    pe.wait_ge(v_split, 2)
                    pe.wait_ge(kv_pads, 6)
                    pe.wait_ge(masks_set, 3)
                    swap_q(0)
                    swap_q(1)
                    for pair in range(4):
                        n, m = 4 * pair, 2 * pair + 2
                        score(n)
                        score(n + 1)
                        if m < DT:
                            project_q(m + 1)
                        turn_p(n)
                        if m < DT:
                            swap_q(m)
                        score(n + 2)
                        turn_p(n + 1)
                        weigh_v(n)
                        if m < DT:
                            swap_q(m + 1)
                        score(n + 3)
                        weigh_v(n + 1)
                        if m + 2 < DT:
                            project_q(m + 2)
                        turn_p(n + 2)
                        turn_p(n + 3)
                        weigh_v(n + 2)
                        weigh_v(n + 3)
                elif ph.kind == "final":
                    def split_ready(k):
                        pe.wait_ge(act_split, ph.tile0 - ph.kt + k + 1)
                    for o in range(DT):
                        group(b0 + o, b0 + o, g0 + o, g0 + o, ph.kt, act_hi, act_lo, tile,
                              ready=split_ready if o == 0 else None)
                    sum_squares(ph.norm0)


LRU_CONST_STEPS = 24


def weight_stream(inputs):
    phases = plan()
    stream = np.zeros((phases[-1].block0 + phases[-1].n_blocks, P, BLK), np.float32)

    def put(block, w, c):
        kt = w.shape[0] // P
        stream[block, :, 0:kt * P] = w[:, c:c + P].reshape(kt, P, P).transpose(1, 0, 2).reshape(P, kt * P)

    for ph in phases:
        if ph.kind == "gu":
            w = inputs["ffn_w_gu"][ph.layer, ph.which]
            for n in range(ph.n_blocks):
                put(ph.block0 + n, w, (ph.first + n // 2) * P + (F if n % 2 else 0))
        elif ph.kind in ("down", "final"):
            w = inputs["ffn_w_down"][ph.layer, ph.which, ph.first * P:(ph.first + ph.kt) * P]
            for n in range(ph.n_blocks):
                put(ph.block0 + n, w, n * P)
        elif ph.kind == "gates":
            for n in range(ph.n_blocks):
                w = inputs["lru_gate_w"][0, :, n]
                stream[ph.block0 + n] = w.reshape(2, 2, P, 2 * P).transpose(2, 0, 1, 3).reshape(P, BLK)
        elif ph.n_blocks:
            w = {"xb": lambda: inputs["lru_w_in"][0][:, 0:D], "yb": lambda: inputs["lru_w_in"][0][:, D:2 * D],
                 "kv": lambda: inputs["w_kv"], "q": lambda: inputs["attn_w_q"][0],
                 "out": lambda: inputs[ph.weight][0]}[ph.kind]()
            for n in range(ph.n_blocks):
                put(ph.block0 + n, w, n * P)
    return stream


def parameter_columns(inputs):
    names = ("ffn_norm", "mix_norm", "kv_norm", "final_norm", "lru_conv_w", "lru_conv_b", "lru_gate_b", "lru_a_param")
    cols = np.concatenate([inputs[k].reshape(-1, P) for k in names]).T
    heads = inputs["attn_sinks"].reshape(4, 2, 2)
    sinks = np.repeat(heads.transpose(1, 0, 2).reshape(2, 8), P // 2, axis=0)
    return np.ascontiguousarray(np.concatenate([cols, sinks], axis=1))


def kernel(**inputs):
    import concourse.bacc as _bacc
    from concourse.bass_utils import run_bass_kernel_spmd as _run

    inputs = {k: np.asarray(v) for k, v in inputs.items()}
    nc = _bacc.Bacc("TRN2", target_bir_lowering=False, num_devices=1)
    arrays, args = {}, []
    for name, a in (("x_dram", np.ascontiguousarray(inputs["x"][0].T.reshape(DT, P, S).transpose(1, 0, 2))),
                    ("params_dram", parameter_columns(inputs)),
                    ("weights_dram", weight_stream(inputs)),
                    ("tables_dram", shape_tables())):
        arrays[name] = a
        args.append(nc.dram_tensor(name, a.shape, F32, kind="ExternalInput").ap())
    args.append(nc.dram_tensor("out_dram", (P, DT, S), F32, kind="ExternalOutput").ap())
    trunk_program(nc, *args)
    r = _run(nc, [arrays], core_ids=[0])
    return np.ascontiguousarray(r.results[0]["out_dram"].transpose(1, 0, 2).reshape(D, S).T[None])
```

```python
from contextlib import ExitStack

import numpy as np

import concourse.bass as bass
from concourse import mybir

F32 = mybir.dt.float32
F32R = mybir.dt.float32r
ALU = mybir.AluOpType
ACT = mybir.ActivationFunctionType
AX_X = mybir.AxisListType.X
ds = bass.ds

P = 128
S = 512
D = 1024
DT = D // P
F = 2816
CHUNK = 64
HEAD = 64
KV_HEADS = 2
ROPE = HEAD // 4
THETA = 500000.0
CONV = 4
EPS = 1e-6
MASK = -2.0 ** 100
BLK = DT * P
RAW = 2
RING = 4
BANKS = 4
PARTS = ((0, 6), (6, 8), (14, 8))
assert sum(n for _, n in PARTS) * P == F

V_FFN, V_MIX, V_KV, V_FINAL, V_CONVW, V_CONVB, V_GATEB, V_A = 0, 32, 48, 56, 64, 96, 104, 120

T_ID, T_SWAP, T_DUP, T_DUPSWAP, T_COS, T_SIN, T_END = 0, 128, 256, 512, 768, 1280, 1792


def shape_tables():
    t = np.zeros((P, T_END), np.float32)
    t[np.arange(P), T_ID + np.arange(P)] = 1.0
    half = ROPE // 2
    for m in range(P):
        d = m % HEAD
        mate = d + half if d < half else d - half
        if d < ROPE:
            t[m - d + mate, T_SWAP + m] = 1.0
        for kv in range(KV_HEADS):
            t[kv * HEAD + d, T_DUP + kv * P + m] = 1.0
            if d < ROPE:
                t[kv * HEAD + mate, T_DUPSWAP + kv * P + m] = 1.0
    inv = np.power(np.float32(THETA), -np.arange(0, ROPE, 2, dtype=np.float32) / np.float32(ROPE)).astype(np.float32)
    ang = np.arange(S, dtype=np.float32)[:, None] * inv[None, :]
    cos, sin = np.cos(ang).T, np.sin(ang).T
    t[:, T_COS:T_COS + S] = 1.0
    for m in range(P):
        d = m % HEAD
        if d < ROPE:
            t[m, T_COS:T_COS + S] = cos[d % half]
            t[m, T_SIN:T_SIN + S] = sin[d % half] * (-1.0 if d < half else 1.0)
    return t


BATCHES = 16
attention_steps = range(-2, BATCHES + 1)


def tile_in_work(s):
    return (s + 6) // 2, s % 2


class Phase:

    def __init__(self, kind, at, blocks, tiles, kt, first, layer, which, gains, scale, weight):
        self.kind = kind
        self.n_blocks = blocks
        self.tiles = tiles
        self.kt = kt
        self.first = first
        self.layer, self.which = layer, which
        self.gains = gains
        self.scale = scale
        self.weight = weight
        self.block0, self.group0, self.tile0, self.product0, self.ff0, self.norm0, self.hg0 = at


def plan():
    phases = []

    def add(kind, blocks, groups, splits=0, products=0, tiles=0, kt=DT, first=0, layer=0, which=0, gains=(),
            scale=1.0, weight=""):
        at = (0,) * 7 if not phases else ends[-1]
        phases.append(Phase(kind, at, blocks, tiles, kt, first, layer, which, gains, scale, weight))
        normed = 1 if gains else 0
        steps = (blocks, groups, splits, products, tiles, normed, DT * len(gains))
        ends.append(tuple(a + b for a, b in zip(at, steps)))

    ends = []

    def ffn(layer, which, gains):
        for n, (first, tiles) in enumerate(PARTS):
            add("gu", 2 * tiles, 2 * tiles, tiles, tiles, tiles, first=first, layer=layer, which=which)
            last = n == len(PARTS) - 1
            add("final" if last and not gains else "down", DT, DT, kt=tiles, first=first, layer=layer, which=which,
                gains=gains if last else (), scale=0.5)

    add("input", 0, 0, gains=((V_FFN, 0),))
    ffn(0, 0, ((V_MIX, 0),))
    add("xb", DT, DT, DT, DT)
    add("gates", 4, 16, kt=2)
    add("yb", DT, DT, DT, DT)
    add("out", DT, DT, gains=((V_FFN + 8, 0),), weight="lru_w_out")
    ffn(0, 1, ((V_KV, 1), (V_FFN + 16, 0)))
    add("kv", 2, 2)
    ffn(1, 0, ((V_MIX + 8, 0),))
    add("q", DT, DT, 2 * DT)
    add("out", DT, DT, gains=((V_FFN + 24, 0),), weight="attn_w_o")
    ffn(1, 1, ())
    return phases


def trunk_program(nc, x, params, weights, tables, out):
    phases = plan()
    n_blocks = phases[-1].block0 + phases[-1].n_blocks

    with ExitStack() as ctx:
        def sb(name, shape, dt=F32, where=ctx):
            return where.enter_context(nc.sbuf_tensor(name, shape, dt))

        def sem(name):
            return ctx.enter_context(nc.semaphore(name))

        h = sb("h", [P, DT, S])
        hg_hi = sb("hg_hi", [P, DT, S], F32R)
        hg_lo = sb("hg_lo", [P, DT, S], F32R)
        act_hi = sb("act_hi", [P, DT, S], F32R)
        act_lo = sb("act_lo", [P, DT, S], F32R)
        raw = sb("raw", [P, RAW, BLK])
        w_hi = sb("w_hi", [P, RING, BLK], F32R)
        w_lo = sb("w_lo", [P, RING, BLK], F32R)
        rstd = sb("rstd", [P, S])
        sqsum = sb("sqsum", [P, S])
        sq = sb("sq", [P, 2, S])
        tmp = sb("tmp", [P, 4, S])
        tab = sb("tab", [P, T_END])
        vec = sb("vec", [P, P + 8])
        ones_r = sb("ones_r", [P, P], F32R)
        ones = ones_r[:, :].bitcast(F32)
        mask = sb("mask", [P, 2 * P], F32R)
        eps = sb("eps", [P, 1])
        warm = sb("warm", [P, 1])
        root4 = sb("root4", [P, S // P])
        lc = sb("lc", [P, 12, DT])
        half_gate_b = sb("half_gate_b", [P, 2 * DT])
        stat = sb("stat", [P, 2, 7, 4])

        with ExitStack() as part:
            lru_r = sb("lru_r", [P, DT, S], where=part)
            lru_i = sb("lru_i", [P, DT, S], where=part)
            lru_x = sb("lru_x", [P, DT, S], where=part)
            xpad = sb("xpad", [P, 2, CONV - 1 + S + 1], where=part)
            th = sb("th", [P, 2, S], where=part)
            asq = sb("asq", [P, 2, S], where=part)
        with ExitStack() as part:
            hkv_hi = sb("hkv_hi", [P, DT, S], F32R, where=part)
            hkv_lo = sb("hkv_lo", [P, DT, S], F32R, where=part)
        with ExitStack() as part:
            v_hi = sb("v_hi", [P, 8, KV_HEADS, 2, HEAD], F32R, where=part)
            v_lo = sb("v_lo", [P, 8, KV_HEADS, 2, HEAD], F32R, where=part)
            k_hi = sb("k_hi", [P, KV_HEADS, 2, CHUNK + S], F32R, where=part)
            k_lo = sb("k_lo", [P, KV_HEADS, 2, CHUNK + S], F32R, where=part)
            q_hi = sb("q_hi", [P, 2, 8, 2, CHUNK], F32R, where=part)
            q_lo = sb("q_lo", [P, 2, 8, 2, CHUNK], F32R, where=part)
            with ExitStack() as early:
                k_f32 = sb("k_f32", [P, S], where=early)
                v_pad = sb("v_pad", [P, CHUNK + S], where=early)
            pt_hi = sb("pt_hi", [P, 2, 4, P], F32R, where=part)
            pt_lo = sb("pt_lo", [P, 2, 4, P], F32R, where=part)

        bank = [ctx.enter_context(nc.psum_tensor(f"bank{n}", [P, S], F32)) for n in range(8)]

        prob = sq[:, :, :].rearrange("p b (u k) -> p b u k", u=4)
        sink = vec[:, P:P + 8].rearrange("p (r f) -> p r f", f=2)

        raw_loaded = [sem(f"raw_loaded{n}") for n in range(RAW)]
        x_loaded = [sem(f"x_loaded{t}") for t in range(DT)]
        params_loaded = sem("params_loaded")
        tables_loaded = sem("tables_loaded")
        consts_set = sem("consts_set")
        masks_set = sem("masks_set")
        lru_const = sem("lru_const")
        lru_const_exp = sem("lru_const_exp")
        w_rounded = sem("w_rounded")
        w_ready = sem("w_ready")
        group_done = sem("group_done")
        drained = sem("drained")
        silu_done = sem("silu_done")
        act_product = sem("act_product")
        act_rounded = sem("act_rounded")
        act_split = sem("act_split")
        squared = sem("squared")
        sq_summed = sem("sq_summed")
        hg_rounded = sem("hg_rounded")
        hg_split = sem("hg_split")
        rms_summed = sem("rms_summed")
        rooted = sem("rooted")
        rstd_ready = sem("rstd_ready")
        conv_started = sem("conv_started")
        conv_step = sem("conv_step")
        lru_decay = sem("lru_decay")
        lru_ix = sem("lru_ix")
        lru_m2 = sem("lru_m2")
        lru_root = sem("lru_root")
        lru_u = sem("lru_u")
        lru_scanned = sem("lru_scanned")
        lru_gelu = sem("lru_gelu")
        kv_pads = sem("kv_pads")
        k_picked = sem("k_picked")
        k_step = sem("k_step")
        k_rounded = sem("k_rounded")
        k_split = sem("k_split")
        v_turned = sem("v_turned")
        v_rounded = sem("v_rounded")
        v_split = sem("v_split")
        q_swapped = sem("q_swapped")
        q_step = sem("q_step")
        q_rounded = sem("q_rounded")
        q_split = sem("q_split")
        scored = sem("scored")
        soft_step = sem("soft_step")
        norm_step = sem("norm_step")
        exped = sem("exped")
        probs_ready = sem("probs_ready")
        p_turned = sem("p_turned")
        p_rounded = sem("p_rounded")
        p_split = sem("p_split")
        pv_done = sem("pv_done")
        out_ready = sem("out_ready")
        stored = sem("stored")

        m2 = [tmp[:, t, :] for t in range(4)] + [sq[:, t, :] for t in range(2)] + [xpad[:, t, 0:S] for t in range(2)]
        gates = next(ph for ph in phases if ph.kind == "gates")

        block = ctx.enter_context(nc.Block())

        def q_places(ph):
            turned = (bank[6], bank[(ph.group0 + 2) % BANKS])

            def swap_bank(m):
                return bank[(ph.group0 + 3) % BANKS]

            def t_bank(n):
                return turned[n % 2]

            def o_views(n, half, act):
                rows, pair, cp = slice(half * HEAD, (half + 1) * HEAD), n // 4, n % 4
                dst = act[rows, 2 * pair:2 * pair + 2, cp * P:(cp + 1) * P].rearrange("p t (c q) -> p c t q", c=2)
                src = bank[7][rows, :].rearrange("p (c f t q) -> p c f t q", c=2, f=2, t=2)[:, :, half]
                return dst, src
            return t_bank, o_views, swap_bank

        def nothing():
            pass

        @block.sync
        def _(sp):
            def load(b, n, k_tiles, first=False):
                if not first:
                    sp.wait_ge(w_ready, b - (RAW - 1))
                sp.dma_start(raw[:, n % RAW, 0:k_tiles * P],
                             weights[ds(b, 1), :, 0:k_tiles * P].rearrange("a p c -> (a p) c")
                             ).then_inc(raw_loaded[n % RAW], 16)

            load(0, 0, DT, first=True)
            for t in range(1, DT, 2):
                sp.dma_start(h[:, t, :], x[:, t, :]).then_inc(x_loaded[t], 16)
            for n in range(1, RAW):
                load(n, n, DT, first=True)
            for ph in phases:
                k_tiles = ph.kt if ph.kind in ("down", "final") else DT
                start = RAW if ph.block0 == 0 else 0
                if ph.n_blocks > start:
                    with sp.Fori(0, (ph.n_blocks - start) // RAW) as i:
                        for j in range(RAW):
                            load(ph.block0 + start + RAW * i + j, ph.block0 + start + j, k_tiles)

        @block.gpsimd
        def _(pool):
            nc.gpsimd.memset(ones_r[:, :].bitcast(F32), 1.0).then_inc(consts_set, 1)
            nc.gpsimd.memset(mask[:, :].bitcast(F32), 0.0).then_inc(masks_set, 1)
            pool.wait_ge(masks_set, 1)
            for half in range(2):
                nc.gpsimd.memset(mask[0:1, half * P:half * P + CHUNK].bitcast(F32), MASK).then_inc(masks_set, 1)
            nc.gpsimd.memset(eps[:, :], EPS).then_inc(consts_set, 1)
            kv = next(ph for ph in phases if ph.kind == "kv")
            pool.wait_ge(group_done, kv.group0 + 2)
            pads = 0
            for t in (k_hi, k_lo):
                for zero in (t[:, :, :, 0:CHUNK], t[HEAD:P, :, 0, CHUNK:CHUNK + S], t[0:HEAD, :, 1, CHUNK:CHUNK + S]):
                    if pads:
                        pool.wait_ge(kv_pads, pads)
                    nc.gpsimd.memset(zero.bitcast(F32), 0.0).then_inc(kv_pads, 1)
                    pads += 1

        @block.scalar
        def _(act):
            def round_weights(b, n, group):
                if n + RING >= n_blocks:
                    return
                if group is not None:
                    act.wait_ge(group_done, group + 1)
                act.wait_ge(raw_loaded[n % RAW], (b - n) * (16 // RAW) + 16 * ((n + RING) // RAW + 1))
                slot = (n + RING) % RING
                nc.scalar.activation(w_hi[:, slot, :], raw[:, (n + RING) % RAW, :], ACT.Copy).then_inc(w_rounded, 1)

            def square(ph, o, j):
                act.wait_ge(sq_summed, 9 * ph.norm0 + o)
                nc.scalar.activation(sq[:, j % 2, :], h[:, o, :], ACT.Square).then_inc(squared, 1)

            def gain_head(ph, o):
                for gain, dest in ph.gains:
                    hi = (hkv_hi if dest else hg_hi)
                    nc.scalar.activation(hi[:, o, :], h[:, o, :], ACT.Copy,
                                         scale=vec[:, ds(gain + o, 1)]).then_inc(hg_rounded, 1)

            def root(norm):
                act.wait_ge(rms_summed, norm + 1)
                nc.scalar.activation(rstd[:, :], bank[4][:, :], ACT.Sqrt, bias=eps[:, 0:1],
                                     scale=1.0 / D).then_inc(rooted, 1)

            def decay(t):
                act.wait_ge(drained, gates.group0 + 4 * (t // 2) + t % 2 + 1)
                if t >= 2:
                    act.wait_ge(lru_m2, t - 1)
                nc.scalar.activation(th[:, t % 2, :], lru_r[:, t, :], ACT.Tanh, bias=lc[:, 10, t:t + 1],
                                     scale=lc[:, 10, t:t + 1]).then_inc(lru_decay, 1)
                nc.scalar.activation(lru_r[:, t, :], lru_r[:, t, :], ACT.Exp, bias=lc[:, 11, t:t + 1],
                                     scale=lc[:, 11, t:t + 1]).then_inc(lru_decay, 1)
                act.wait_ge(lru_decay, 3 * t + 2)
                nc.scalar.activation(asq[:, t % 2, :], lru_r[:, t, :], ACT.Square).then_inc(lru_decay, 1)

            def split_k(kv):
                act.wait_ge(k_step, 3 * (kv + 1))
                for half in range(2):
                    rows = slice(half * HEAD, (half + 1) * HEAD)
                    nc.scalar.activation(k_hi[rows, kv, half, CHUNK:CHUNK + S], sq[rows, 1, :],
                                         ACT.Copy).then_inc(k_rounded, 1)

            def split_v(n):
                act.wait_ge(v_turned, n + 1)
                for dup in range(2):
                    nc.scalar.activation(v_hi[:, 4 * n:4 * n + 4, :, dup, :].rearrange("p c v d -> p (c v) d"),
                                         bank[4 + n][:, :].rearrange("p (c d) -> p c d", d=HEAD),
                                         ACT.Copy).then_inc(v_rounded, 1)

            act.dma_start(vec[:, :], params).then_inc(params_loaded, 16)
            for t in range(0, DT, 2):
                act.dma_start(h[:, t, :], x[:, t, :]).then_inc(x_loaded[t], 16)
            act.dma_start(tab[:, :], tables).then_inc(tables_loaded, 16)
            act.wait_ge(consts_set, 1)
            nc.scalar.activation(warm[:, :], ones[:, 0:1], ACT.Copy)

            for idx, ph in enumerate(phases):
                b0, g0 = ph.block0, ph.group0
                if ph.kind == "input":
                    act.wait_ge(params_loaded, 16)
                    for o in range(DT):
                        act.wait_ge(x_loaded[o], 16)
                        gain_head(ph, o)
                        if o == 0:
                            round_weights(-RING, -RING, None)
                    round_weights(1 - RING, 1 - RING, None)
                    for o in range(DT):
                        square(ph, o, o)
                        if o in (3, 7):
                            round_weights(2 + o // 4 - RING, 2 + o // 4 - RING, None)
                    act.wait_ge(consts_set, 2)
                    root(ph.norm0)
                elif ph.kind == "gu":
                    def ffn_tiles(i, after=()):
                        for j in range(4):
                            if j % 2 == 0:
                                act.wait_ge(drained, g0 + 4 * i + j + 1)
                                nc.scalar.activation(tmp[:, 1, :], tmp[:, 0, :], ACT.Silu).then_inc(silu_done, 1)
                            round_weights(b0 + 4 * i + j, b0 + j, g0 + 4 * i + j)
                            if j % 2 == 1:
                                act.wait_ge(act_product, ph.product0 + 2 * i + j // 2 + 1)
                                nc.scalar.activation(act_hi[:, 2 * i + j // 2, :], tmp[:, 3, :],
                                                     ACT.Copy).then_inc(act_rounded, 1)
                            if j < len(after):
                                after[j]()
                    def decay_exp():
                        act.wait_ge(lru_const, 2)
                        nc.scalar.activation(lc[:, 2, :], lc[:, 1, :], ACT.Exp, scale=-1.0).then_inc(lru_const_exp, 1)

                    start = 0
                    if phases[idx - 1].kind == "input":
                        ffn_tiles(0, (nothing, nothing, nothing, decay_exp))
                        start = 1
                    if phases[idx - 1].kind == "kv":
                        ffn_tiles(0, (lambda: (split_k(0), split_k(1)), lambda: (split_v(0), split_v(1))))
                        start = 1
                    with act.Fori(start, ph.tiles // 2) as i:
                        ffn_tiles(i)
                elif ph.kind == "down" or ph.kind == "out":
                    with act.Fori(0, DT // 4) as i:
                        for j in range(4):
                            o = 4 * i + j
                            round_weights(b0 + o, b0 + j, g0 + o)
                            if ph.gains:
                                act.wait_ge(drained, g0 + o + 1)
                                square(ph, o, j)
                            gain_head(ph, o)
                    if ph.gains:
                        root(ph.norm0)
                elif ph.kind == "xb":
                    def head_of_x(t, first=ph.product0):
                        act.wait_ge(act_product, first + t + 1)
                        nc.scalar.activation(act_hi[:, t, :], lru_x[:, t, :], ACT.Copy).then_inc(act_rounded, 1)

                    def xb_tiles(i, last):
                        for j in range(4):
                            t = 4 * i + j
                            act.wait_ge(drained, g0 + t + 1)
                            nc.scalar.activation(lru_x[:, t, :], xpad[:, j % 2, 0:S], ACT.Identity,
                                                 bias=vec[:, ds(V_CONVB + t, 1)],
                                                 scale=vec[:, ds(V_CONVW + t, 1)]).then_inc(conv_started, 1)
                            round_weights(b0 + t, b0 + j, g0 + t)
                            if not (last and j == 3):
                                head_of_x(t)
                    with act.Fori(0, DT // 4 - 1) as i:
                        xb_tiles(i, False)
                    xb_tiles(DT // 4 - 1, True)
                elif ph.kind == "gates":
                    for hb in range(4):
                        for n in range(4):
                            g, t = n // 2, 2 * hb + n % 2
                            if hb == 0 and n == 0:
                                act.wait_ge(drained, g0)
                                act.wait_ge(lru_const, LRU_CONST_STEPS)
                            act.wait_ge(group_done, g0 + 4 * hb + n + 1)
                            nc.scalar.activation((lru_i if g else lru_r)[:, t, :], bank[(g0 + n) % BANKS][:, :],
                                                 ACT.Tanh, bias=half_gate_b[:, 8 * g + t:8 * g + t + 1],
                                                 scale=0.5).then_inc(drained, 1)
                        if hb == 0:
                            head_of_x(DT - 1)
                        round_weights(b0 + hb, b0 + hb, g0 + 4 * hb + 3)
                        if hb:
                            decay(hb - 1)
                    decay(3)
                elif ph.kind == "yb":
                    def root_m2(t):
                        act.wait_ge(lru_m2, t + 1)
                        nc.scalar.activation(m2[t], m2[t], ACT.Sqrt).then_inc(lru_root, 1)

                    def gelu(t):
                        act.wait_ge(drained, g0 + t + 1)
                        nc.scalar.activation(lru_x[:, t, :], lru_x[:, t, :], ACT.Gelu_apprx_tanh).then_inc(lru_gelu, 1)

                    def head_of_y(t):
                        act.wait_ge(act_product, ph.product0 + t + 1)
                        nc.scalar.activation(act_hi[:, t, :], tmp[:, t % 4, :], ACT.Copy).then_inc(act_rounded, 1)

                    roots = lambda first: [(root_m2, t) for t in range(first, first + 4)]
                    beside = ([(decay, 4), (decay, 5)], roots(0), [(decay, 6), (decay, 7)],
                              roots(4) + [(gelu, 0), (gelu, 1)], [(gelu, 2), (gelu, 3), (gelu, 4), (head_of_y, 0)],
                              [(gelu, 5), (head_of_y, 1), (head_of_y, 2), (head_of_y, 3)],
                              [(gelu, 6), (head_of_y, 4), (head_of_y, 5)],
                              [(gelu, 7), (head_of_y, 6), (head_of_y, 7)])
                    for s in range(DT):
                        if s < DT - 1:
                            round_weights(b0 + s, b0 + s, g0 + s)
                        for what, t in beside[s]:
                            what(t)
                    round_weights(b0 + DT - 1, b0 + DT - 1, g0 + DT - 1)
                elif ph.kind == "kv":
                    for j in range(2):
                        round_weights(b0 + j, b0 + j, g0 + j)
                elif ph.kind == "q":
                    def head_of_q(m):
                        act.wait_ge(q_step, 3 * (m + 1))
                        nc.scalar.activation(q_hi[:, (m // 2) % 2, :, m % 2, :],
                                             tmp[:, 2, :].rearrange("p (c q) -> p c q", q=CHUNK),
                                             ACT.Copy).then_inc(q_rounded, 1)

                    def exps(n):
                        par = n % 2
                        act.wait_ge(soft_step, 4 * (n + 1))
                        for u in range(4):
                            nc.scalar.activation(prob[:, par, u, :], bank[4 + par][:, u * P:(u + 1) * P], ACT.Exp,
                                                 bias=stat[:, par, 1, u:u + 1], scale=HEAD ** -0.5,
                                                 accum_out=stat[:, par, 4, u:u + 1])
                        nc.scalar.activation(stat[:, par, 3, :], stat[:, par, 2, :], ACT.Exp).then_inc(exped, 1)

                    def head_of_p(n):
                        act.wait_ge(p_turned, n + 1)
                        nc.scalar.activation(pt_hi[:, n % 2, :, :].rearrange("p u q -> p (u q)"), t_bank(n)[:, :],
                                             ACT.Copy).then_inc(p_rounded, 1)

                    def head_of_o(n):
                        act.wait_ge(pv_done, n + 1)
                        for half in range(2):
                            dst, src = o_views(n, half, act_hi)
                            ins = nc.scalar.activation(dst, src, ACT.Copy)
                        ins.then_inc(act_rounded, 1)

                    t_bank, o_views, swap_bank = q_places(ph)

                    def round_q(m):
                        round_weights(b0 + m, b0 + m, g0 + m)

                    for m in range(2):
                        round_q(m)
                    for m in range(2):
                        head_of_q(m)
                    for s in attention_steps:
                        m, part = tile_in_work(s)
                        if 0 <= s < BATCHES:
                            head_of_p(s)
                        if s >= 1:
                            head_of_o(s - 1)
                        if m < DT and part == 0:
                            round_q(m)
                        if m < DT and part == 1:
                            head_of_q(m)
                        if s + 2 < BATCHES:
                            exps(s + 2)
                elif ph.kind == "final":
                    for o in range(DT):
                        round_weights(b0 + o, b0 + o, g0 + o)
                        act.wait_ge(drained, g0 + o + 1)
                        square(ph, o, o)
                        if o == DT - 2:
                            nc.scalar.activation(warm[:, :], ones[:, 0:1], ACT.Sqrt)
                    act.wait_ge(rms_summed, ph.norm0 + 1)
                    nc.scalar.activation(root4[:, :], bank[4][:, 0:S // P], ACT.Sqrt, bias=eps[:, 0:1],
                                         scale=1.0 / D).then_inc(rooted, 1)
                    for t in range(DT):
                        act.wait_ge(out_ready, t + 1)
                        act.dma_start(out[:, t, :], h[:, t, :]).then_inc(stored, 16)
                    act.wait_ge(stored, 16 * DT)

        @block.vector
        def _(dve):
            def split_weights(b, n):
                if n + RING >= n_blocks:
                    return
                dve.wait_ge(w_rounded, b + RING + 1)
                slot = (n + RING) % RING
                nc.vector.tensor_tensor(w_lo[:, slot, :], raw[:, (n + RING) % RAW, :],
                                        w_hi[:, slot, :].bitcast(F32), ALU.subtract).then_inc(w_ready, 1)

            def residual_open(ph):
                nc.vector.memset(sqsum[:, :], 0.0).then_inc(sq_summed, 1)

            def add_square(ph, o, j):
                dve.wait_ge(squared, DT * ph.norm0 + o + 1)
                dve.wait_ge(sq_summed, 9 * ph.norm0 + o + 1)
                nc.vector.tensor_tensor(sqsum[:, :], sqsum[:, :], sq[:, j % 2, :], ALU.add).then_inc(sq_summed, 1)

            def gain_rest(ph, o):
                for n, (gain, dest) in enumerate(ph.gains):
                    hi, lo = (hkv_hi, hkv_lo) if dest else (hg_hi, hg_lo)
                    dve.wait_ge(hg_rounded, ph.hg0 + len(ph.gains) * o + n + 1)
                    nc.vector.scalar_tensor_tensor(lo[:, o, :], h[:, o, :], vec[:, ds(gain + o, 1)],
                                                   hi[:, o, :].bitcast(F32), ALU.mult,
                                                   ALU.subtract).then_inc(hg_split, 1)

            def invert(norm):
                dve.wait_ge(rooted, norm + 1)
                nc.vector.reciprocal(rstd[:, :], rstd[:, :]).then_inc(rstd_ready, 1)
                dve.wait_ge(rstd_ready, norm + 1)

            def drain_scaled(dst, g, n):
                dve.wait_ge(group_done, g + 1)
                nc.vector.tensor_tensor(dst, bank[n % BANKS][:, :], rstd[:, :], ALU.mult).then_inc(drained, 1)

            def rest(t, src, count):
                dve.wait_ge(act_rounded, count + 1)
                nc.vector.tensor_tensor(act_lo[:, t, :], src, act_hi[:, t, :].bitcast(F32),
                                        ALU.subtract).then_inc(act_split, 1)

            def gated_input(t):
                dve.wait_ge(drained, gates.group0 + 4 * (t // 2) + 2 + t % 2 + 1)
                nc.vector.scalar_tensor_tensor(lru_i[:, t, :], lru_i[:, t, :], 1.0, lru_x[:, t, :], ALU.add,
                                               ALU.mult).then_inc(lru_ix, 1)

            def decay_rest(t):
                dve.wait_ge(lru_decay, 3 * (t + 1))
                nc.vector.scalar_tensor_tensor(m2[t], asq[:, t % 2, :], 1.0, th[:, t % 2, :], ALU.add,
                                               ALU.mult).then_inc(lru_m2, 1)

            lc_steps = [0]

            def lc_op(ins):
                lc_steps[0] += 1
                ins.then_inc(lru_const, 1)
                dve.wait_ge(lru_const, lc_steps[0])

            def lru_constants():
                a = vec[:, V_A:V_A + DT]
                c = lambda n: lc[:, n, :]
                lc_op(nc.vector.tensor_scalar(c(0), a, -1.0, None, ALU.mult))
                lc_op(nc.vector.tensor_tensor(c(1), a, c(0), ALU.max))
                dve.wait_ge(lru_const_exp, 1)
                lc_op(nc.vector.tensor_scalar(c(3), c(2), 2.0, None, ALU.add))
                lc_op(nc.vector.reciprocal(c(4), c(3)))
                lc_op(nc.vector.tensor_tensor(c(5), c(2), c(4), ALU.mult))
                lc_op(nc.vector.tensor_tensor(c(6), c(5), c(5), ALU.mult))
                lc_op(nc.vector.tensor_scalar(c(7), c(6), 1.0 / 15, 1.0 / 13, ALU.mult, ALU.add))
                for k in (11, 9, 7, 5, 3, 1):
                    lc_op(nc.vector.tensor_tensor(c(7), c(7), c(6), ALU.mult))
                    lc_op(nc.vector.tensor_scalar(c(7), c(7), 1.0 / k, None, ALU.add))
                lc_op(nc.vector.tensor_tensor(c(7), c(7), c(5), ALU.mult))
                lc_op(nc.vector.tensor_scalar(c(8), c(0), 0.0, None, ALU.max))
                lc_op(nc.vector.scalar_tensor_tensor(c(9), c(7), 2.0, c(8), ALU.mult, ALU.add))
                lc_op(nc.vector.tensor_scalar(c(10), c(9), 4.0, None, ALU.mult))
                lc_op(nc.vector.tensor_scalar(c(11), c(9), -4.0, None, ALU.mult))
                lc_op(nc.vector.tensor_scalar(half_gate_b[:, :], vec[:, V_GATEB:V_GATEB + 2 * DT], 0.5, None, ALU.mult))
                assert lc_steps[0] == LRU_CONST_STEPS

            def rotate_k(kv):
                dve.wait_ge(k_picked, kv + 1)
                if kv:
                    dve.wait_ge(k_split, 1)
                nc.vector.tensor_tensor(sq[:, 0, :], bank[4 + 2 * kv][:, :], tab[:, T_COS:T_COS + S],
                                        ALU.mult).then_inc(k_step, 1)
                nc.vector.tensor_tensor(sq[:, 1, :], bank[5 + 2 * kv][:, :], tab[:, T_SIN:T_SIN + S],
                                        ALU.mult).then_inc(k_step, 1)
                dve.wait_ge(k_step, 3 * kv + 2)
                nc.vector.tensor_tensor(sq[:, 1, :], sq[:, 1, :], sq[:, 0, :], ALU.add).then_inc(k_step, 1)
                dve.wait_ge(k_rounded, 2 * kv + 2)
                for half in range(2):
                    rows = slice(half * HEAD, (half + 1) * HEAD)
                    ins = nc.vector.tensor_tensor(k_lo[rows, kv, half, CHUNK:CHUNK + S], sq[rows, 1, :],
                                                  k_hi[rows, kv, half, CHUNK:CHUNK + S].bitcast(F32), ALU.subtract)
                ins.then_inc(k_split, 1)

            def rest_of_v(n):
                dve.wait_ge(v_rounded, 2 * n + 2)
                for dup in range(2):
                    at = (slice(None), slice(4 * n, 4 * n + 4), slice(None), dup, slice(None))
                    ins = nc.vector.tensor_tensor(v_lo[at].rearrange("p c v d -> p (c v) d"),
                                                  bank[4 + n][:, :].rearrange("p (c d) -> p c d", d=HEAD),
                                                  v_hi[at].rearrange("p c v d -> p (c v) d").bitcast(F32),
                                                  ALU.subtract)
                ins.then_inc(v_split, 1)

            for idx, ph in enumerate(phases):
                b0, g0 = ph.block0, ph.group0
                if ph.kind == "input":
                    residual_open(ph)
                    dve.wait_ge(params_loaded, 16)
                    for o in range(DT):
                        gain_rest(ph, o)
                        if o == 0:
                            split_weights(-RING, -RING)
                    split_weights(1 - RING, 1 - RING)
                    for o in range(DT):
                        add_square(ph, o, o)
                        if o in (3, 7):
                            split_weights(2 + o // 4 - RING, 2 + o // 4 - RING)
                    invert(ph.norm0)
                elif ph.kind == "gu":
                    def ffn_tiles(i, after=()):
                        for j in range(4):
                            t = 2 * i + j // 2
                            drain_scaled(tmp[:, 2 if j % 2 else 0, :], g0 + 4 * i + j, g0 + j)
                            if j % 2:
                                dve.wait_ge(silu_done, ph.ff0 + t + 1)
                                dve.wait_ge(drained, g0 + 4 * i + j + 1)
                                nc.vector.tensor_tensor(tmp[:, 3, :], tmp[:, 1, :], tmp[:, 2, :],
                                                        ALU.mult).then_inc(act_product, 1)
                            split_weights(b0 + 4 * i + j, b0 + j)
                            if j % 2:
                                rest(t, tmp[:, 3, :], ph.tile0 + t)
                            if j < len(after):
                                after[j]()
                    start = 0
                    if phases[idx - 1].kind in ("input", "kv"):
                        start = 1
                        ffn_tiles(0, (lambda: (rotate_k(0), rotate_k(1)), lambda: (rest_of_v(0), rest_of_v(1)))
                                  if phases[idx - 1].kind == "kv" else (nothing, nothing, nothing, lru_constants))
                    with dve.Fori(start, ph.tiles // 2) as i:
                        ffn_tiles(i)
                elif ph.kind in ("down", "out"):
                    if ph.gains:
                        residual_open(ph)

                    def residual_tiles(i, first):
                        for j in range(4):
                            o = 4 * i + j
                            dve.wait_ge(group_done, g0 + o + 1)
                            nc.vector.scalar_tensor_tensor(h[:, o, :], bank[(g0 + j) % BANKS][:, :], ph.scale,
                                                           h[:, o, :], ALU.mult, ALU.add).then_inc(drained, 1)
                            if ph.gains and not (first and j == 0):
                                add_square(ph, o - 1, j + 3)
                                gain_rest(ph, o - 1)
                            split_weights(b0 + o, b0 + j)
                    residual_tiles(0, True)
                    with dve.Fori(1, DT // 4) as i:
                        residual_tiles(i, False)
                    if ph.gains:
                        gain_rest(ph, DT - 1)
                        add_square(ph, DT - 1, DT - 1)
                    if ph.gains:
                        invert(ph.norm0)
                elif ph.kind == "xb":
                    nc.vector.memset(xpad[:, :, 0:CONV - 1], 0.0)

                    def tap(i, j, k):
                        t = 4 * i + j
                        if k > 1:
                            dve.wait_ge(conv_step, 2 * t + k - 1)
                        else:
                            dve.wait_ge(conv_started, t + 1)
                        nc.vector.scalar_tensor_tensor(
                            lru_x[:, t, :], xpad[:, j % 2, k:k + S], vec[:, ds(V_CONVW + 8 * k + t, 1)],
                            lru_x[:, t, :], ALU.mult, ALU.add).then_inc(conv_step if k < CONV - 1 else act_product, 1)

                    def xb_tiles(i, first):
                        for j in range(4):
                            t = 4 * i + j
                            drain_scaled(xpad[:, j % 2, CONV - 1:CONV - 1 + S], g0 + t, g0 + j)
                            if not (first and j == 0):
                                rest(t - 1, lru_x[:, t - 1, :], ph.tile0 + t - 1)
                                split_weights(b0 + t - 1, b0 + j + 3)
                            for k in range(1, CONV):
                                tap(i, j, k)
                    xb_tiles(0, True)
                    with dve.Fori(1, DT // 4) as i:
                        xb_tiles(i, False)
                    split_weights(b0 + DT - 1, b0 + DT - 1)
                    rest(DT - 1, lru_x[:, DT - 1, :], ph.tile0 + DT - 1)
                elif ph.kind == "gates":
                    for hb in range(4):
                        split_weights(b0 + hb, b0 + hb)
                        gated_input(2 * hb)
                        gated_input(2 * hb + 1)
                        if hb:
                            decay_rest(hb - 1)
                elif ph.kind == "yb":
                    def scan(t):
                        dve.wait_ge(lru_root, t + 1)
                        dve.wait_ge(lru_ix, t + 1)
                        nc.vector.scalar_tensor_tensor(lru_i[:, t, :], m2[t], 0.5, lru_i[:, t, :],
                                                       ALU.mult, ALU.mult).then_inc(lru_u, 1)
                        dve.wait_ge(lru_u, t + 1)
                        nc.vector.tensor_tensor_scan(lru_r[:, t, :], lru_r[:, t, :], lru_i[:, t, :], 0.0,
                                                     ALU.mult, ALU.add).then_inc(lru_scanned, 1)

                    def product(t):
                        dve.wait_ge(lru_gelu, t + 1)
                        dve.wait_ge(lru_scanned, t + 1)
                        if t >= 4:
                            dve.wait_ge(act_split, ph.tile0 + t - 3)
                        nc.vector.tensor_tensor(tmp[:, t % 4, :], lru_r[:, t, :], lru_x[:, t, :],
                                                ALU.mult).then_inc(act_product, 1)

                    def rest_of_y(t):
                        rest(t, tmp[:, t % 4, :], ph.tile0 + t)

                    beside = ([(decay_rest, 3), (decay_rest, 4)], [(decay_rest, 5), (scan, 0), (scan, 1)],
                              [(scan, 2), (scan, 3), (decay_rest, 6), (decay_rest, 7)], [(scan, 4), (scan, 5)],
                              [(scan, 6), (scan, 7), (product, 0), (rest_of_y, 0)],
                              [(product, 1), (product, 2), (rest_of_y, 1), (product, 3), (rest_of_y, 2),
                               (rest_of_y, 3)],
                              [(product, 4), (product, 5), (rest_of_y, 4), (product, 6), (rest_of_y, 5)],
                              [(rest_of_y, 6), (product, 7), (rest_of_y, 7)])
                    dve.wait_ge(drained, g0)
                    for s in range(DT):
                        drain_scaled(lru_x[:, s, :], g0 + s, g0 + s)
                        if s < DT - 1:
                            split_weights(b0 + s, b0 + s)
                        for what, t in beside[s]:
                            what(t)
                    split_weights(b0 + DT - 1, b0 + DT - 1)
                elif ph.kind == "kv":
                    nc.vector.memset(v_pad[:, 0:CHUNK], 0.0)
                    drain_scaled(k_f32[:, :], g0, g0)
                    split_weights(b0, b0)
                    drain_scaled(v_pad[:, CHUNK:CHUNK + S], g0 + 1, g0 + 1)
                    split_weights(b0 + 1, b0 + 1)
                elif ph.kind == "q":
                    t_bank, o_views, swap_bank = q_places(ph)

                    def drain_q(m):
                        if m >= 2:
                            dve.wait_ge(q_split, m - 1)
                        dve.wait_ge(group_done, g0 + m + 1)
                        nc.vector.tensor_tensor(tmp[:, m % 2, :], bank[(g0 + m % 2) % BANKS][:, :], rstd[:, :],
                                                ALU.mult).then_inc(drained, 1)

                    def split_q(m):
                        split_weights(b0 + m, b0 + m)

                    def cos_q(m):
                        dve.wait_ge(drained, g0 + m + 1)
                        if m:
                            dve.wait_ge(q_split, m)
                        nc.vector.tensor_tensor(tmp[:, 2, :], tmp[:, m % 2, :], tab[:, T_COS:T_COS + S],
                                                ALU.mult).then_inc(q_step, 1)

                    def sin_q(m):
                        dve.wait_ge(q_swapped, m + 1)
                        nc.vector.tensor_tensor(tmp[:, 3, :], swap_bank(m)[:, :], tab[:, T_SIN:T_SIN + S],
                                                ALU.mult).then_inc(q_step, 1)
                        dve.wait_ge(q_step, 3 * m + 2)
                        nc.vector.tensor_tensor(tmp[:, 2, :], tmp[:, 2, :], tmp[:, 3, :],
                                                ALU.add).then_inc(q_step, 1)

                    def rest_of_q(m):
                        dve.wait_ge(q_rounded, m + 1)
                        nc.vector.tensor_tensor(q_lo[:, (m // 2) % 2, :, m % 2, :],
                                                tmp[:, 2, :].rearrange("p (c q) -> p c q", q=CHUNK),
                                                q_hi[:, (m // 2) % 2, :, m % 2, :].bitcast(F32),
                                                ALU.subtract).then_inc(q_split, 1)

                    def maxima(n):
                        par, pair = n % 2, n // 4
                        dve.wait_ge(scored, n + 1)
                        mx, neg, arg = (stat[:, par, r, :] for r in range(3))
                        two = lambda ap: ap.rearrange("p (c f) -> p c f", f=2)
                        sinks = sink[:, pair, :].unsqueeze(1).broadcast_to([P, 2, 2])
                        nc.vector.tensor_reduce(mx, bank[4 + par][:, :].rearrange("p (u k) -> p u k", u=4), AX_X,
                                                ALU.max).then_inc(soft_step, 1)
                        dve.wait_ge(soft_step, 4 * n + 1)
                        nc.vector.scalar_tensor_tensor(two(mx), two(mx), HEAD ** -0.5, sinks, ALU.mult,
                                                       ALU.max).then_inc(soft_step, 1)
                        dve.wait_ge(soft_step, 4 * n + 2)
                        nc.vector.tensor_scalar(neg, mx, -1.0, None, ALU.mult).then_inc(soft_step, 1)
                        nc.vector.tensor_tensor(two(arg), sinks, two(mx), ALU.subtract).then_inc(soft_step, 1)

                    def normalise(n):
                        par = n % 2
                        dve.wait_ge(exped, n + 1)
                        es, sums, den, inv = (stat[:, par, r, :] for r in range(3, 7))
                        nc.vector.tensor_tensor(den, sums, es, ALU.add).then_inc(norm_step, 1)
                        dve.wait_ge(norm_step, 2 * n + 1)
                        nc.vector.reciprocal(inv, den).then_inc(norm_step, 1)
                        dve.wait_ge(norm_step, 2 * n + 2)
                        nc.vector.tensor_tensor(prob[:, par, :, :], prob[:, par, :, :],
                                                inv.unsqueeze(2).broadcast_to([P, 4, P]),
                                                ALU.mult).then_inc(probs_ready, 1)

                    def rest_of_p(n):
                        dve.wait_ge(p_rounded, n + 1)
                        nc.vector.tensor_tensor(pt_lo[:, n % 2, :, :].rearrange("p u q -> p (u q)"), t_bank(n)[:, :],
                                                pt_hi[:, n % 2, :, :].rearrange("p u q -> p (u q)").bitcast(F32),
                                                ALU.subtract).then_inc(p_split, 1)

                    def rest_of_o(n):
                        dve.wait_ge(act_rounded, ph.tile0 + n + 1)
                        for half in range(2):
                            dst, src = o_views(n, half, act_lo)
                            hi, _ = o_views(n, half, act_hi)
                            ins = nc.vector.tensor_tensor(dst, src, hi.bitcast(F32), ALU.subtract)
                        ins.then_inc(act_split, 1)

                    for m in range(2):
                        drain_q(m)
                        split_q(m)
                    for m in range(2):
                        cos_q(m)
                        sin_q(m)
                        rest_of_q(m)
                    for s in attention_steps:
                        m, part = tile_in_work(s)
                        if 0 <= s < BATCHES:
                            rest_of_p(s)
                        if m < DT and part == 0:
                            drain_q(m)
                        if m < DT and part == 1:
                            sin_q(m)
                        if s >= 1:
                            rest_of_o(s - 1)
                        if s + 2 < BATCHES:
                            maxima(s + 2)
                        if m < DT and part == 0:
                            cos_q(m)
                            split_q(m)
                        if m < DT and part == 1:
                            rest_of_q(m)
                        if s + 2 < BATCHES:
                            normalise(s + 2)
                elif ph.kind == "final":
                    residual_open(ph)
                    for o in range(DT):
                        dve.wait_ge(group_done, g0 + o + 1)
                        nc.vector.scalar_tensor_tensor(h[:, o, :], bank[(g0 + o) % BANKS][:, :], ph.scale,
                                                       h[:, o, :], ALU.mult, ALU.add).then_inc(drained, 1)
                        if o < DT - 1:
                            add_square(ph, o, o)
                        split_weights(b0 + o, b0 + o)
                    dve.wait_ge(rooted, ph.norm0 + 1)
                    nc.vector.reciprocal(root4[:, :], root4[:, :]).then_inc(rstd_ready, 1)
                    dve.wait_ge(rstd_ready, ph.norm0 + 1)
                    nc.vector.tensor_tensor(tmp[:, 0, :].rearrange("p (c q) -> p c q", q=P),
                                            tab[:, T_ID:T_ID + P].unsqueeze(1).broadcast_to([P, S // P, P]),
                                            root4[:, :].unsqueeze(2).broadcast_to([P, S // P, P]),
                                            ALU.mult).then_inc(rstd_ready, 1)
                    dve.wait_ge(rms_summed, ph.norm0 + 2)
                    for t in range(DT):
                        nc.vector.scalar_tensor_tensor(h[:, t, :], h[:, t, :], vec[:, V_FINAL + t:V_FINAL + t + 1],
                                                       bank[5][:, :], ALU.mult, ALU.mult).then_inc(out_ready, 1)

        @block.tensor
        def _(pe):
            def group(b, n_slot, g, n_bank, k_tiles, x_hi, x_lo, w_tile, ready=None, wait_block=True, part=None):
                if wait_block:
                    pe.wait_ge(w_ready, b + 1)
                if n_bank >= BANKS:
                    pe.wait_ge(drained, g + 1 - BANKS)
                dst = bank[n_bank % BANKS][:, :]
                slot = n_slot % RING
                for k in part or range(k_tiles):
                    if ready is not None:
                        ready(k)
                    nc.tensor.matmul(dst, w_tile(w_hi, slot, k), x_hi[:, k, :], start=(k == 0), stop=False)
                    nc.tensor.matmul(dst, w_tile(w_hi, slot, k), x_lo[:, k, :], start=False, stop=False)
                    mm = nc.tensor.matmul(dst, w_tile(w_lo, slot, k), x_hi[:, k, :], start=False,
                                          stop=(k == k_tiles - 1))
                if k == k_tiles - 1:
                    mm.then_inc(group_done, 1)

            def tile(w, slot, k):
                return w[:, slot, k * P:(k + 1) * P]

            def sum_squares(norm):
                pe.wait_ge(sq_summed, 9 * (norm + 1))
                nc.tensor.matmul(bank[4][:, :], ones, sqsum[:, :], start=True, stop=True).then_inc(rms_summed, 1)

            ident = tab[:, T_ID:T_ID + P]
            pending = []

            def run(ph, n, one):
                start = 0
                if pending:
                    for j in range(4):
                        one(0, j)
                        what = pending.pop(0) if pending else None
                        if what is not None:
                            what()
                    start = 1
                if n // 4 > start:
                    with pe.Fori(start, n // 4) as i:
                        for j in range(4):
                            one(i, j)

            for idx, ph in enumerate(phases):
                b0, g0 = ph.block0, ph.group0
                ph_gains = next((len(q.gains) for q in reversed(phases[:idx]) if q.gains), 1)

                def hg_ready(k):
                    pe.wait_ge(hg_split, ph.hg0 - DT * ph_gains + (k + 1) * ph_gains)

                if ph.kind == "input":
                    pe.wait_ge(consts_set, 2)
                    pending += [None, lambda n=ph.norm0: sum_squares(n)]
                elif ph.kind in ("gu", "xb", "yb"):
                    def one(i, j):
                        group(b0 + 4 * i + j, b0 + j, g0 + 4 * i + j, g0 + j, DT, hg_hi, hg_lo, tile,
                              ready=hg_ready if j == 0 else None)
                    run(ph, ph.n_blocks, one)
                elif ph.kind in ("down", "out"):
                    def split_ready(k):
                        pe.wait_ge(act_split, ph.tile0 - ph.kt + k + 1)
                    def one(i, j):
                        group(b0 + 4 * i + j, b0 + j, g0 + 4 * i + j, g0 + j, ph.kt, act_hi, act_lo, tile,
                              ready=split_ready if j == 0 else None)
                    if ph.weight == "attn_w_o":
                        run_to = []
                        for o in (2, 0, 1, 2, 3):
                            ks = range(DT - 2) if o == 2 and not run_to else range(DT - 2, DT)
                            run_to.append(o)
                            if ks[0]:
                                pe.wait_ge(act_split, ph.tile0)
                            group(b0 + o, b0 + o, g0 if not ks[0] else g0 + o, g0 + o, DT, act_hi, act_lo, tile,
                                  part=ks)
                        with pe.Fori(1, DT // 4) as i:
                            for j in range(4):
                                one(i, j)
                    else:
                        run(ph, DT, one)
                    if ph.gains:
                        if phases[idx + 1].kind == "gu":
                            pending.append(None)
                        pending.append(lambda n=ph.norm0: sum_squares(n))
                elif ph.kind == "gates":
                    xb = phases[idx - 1]
                    for hb in range(4):
                        for n in range(4):
                            g, ot = n // 2, n % 2

                            def gate_tile(w, slot, k):
                                at = g * 512 + k * 256 + ot * P
                                return w[:, slot, at:at + P]

                            def xc_ready(k):
                                pe.wait_ge(act_split, xb.tile0 + 2 * hb + k + 1)
                            group(b0 + hb, b0 + hb, g0 + 4 * hb + n, g0 + n, 2, act_hi[:, 2 * hb:2 * hb + 2, :],
                                  act_lo[:, 2 * hb:2 * hb + 2, :], gate_tile, ready=xc_ready, wait_block=(n == 0))
                elif ph.kind == "kv":
                    for j in range(2):
                        group(b0 + j, b0 + j, g0 + j, g0 + j, DT, hkv_hi, hkv_lo, tile, ready=hg_ready)
                        if j == 0:
                            pending.pop(0)()

                    def pick_k(g=g0):
                        pe.wait_ge(tables_loaded, 16)
                        pe.wait_ge(drained, g + 1)
                        for kv in range(KV_HEADS):
                            nc.tensor.matmul(bank[4 + 2 * kv][:, :], tab[:, T_DUP + kv * P:T_DUP + (kv + 1) * P],
                                             k_f32[:, :], start=True, stop=True)
                            nc.tensor.matmul(bank[5 + 2 * kv][:, :],
                                             tab[:, T_DUPSWAP + kv * P:T_DUPSWAP + (kv + 1) * P], k_f32[:, :], start=True,
                                             stop=True).then_inc(k_picked, 1)

                    def turn_v(g=g0):
                        pe.wait_ge(drained, g + 2)
                        pe.wait_ge(k_step, 2)
                        for n in range(2):
                            for c in range(4):
                                t0 = (4 * n + c) * CHUNK
                                mm = nc.tensor.transpose(bank[4 + n][:, c * P:(c + 1) * P], v_pad[:, t0:t0 + P],
                                                         ident)
                            mm.then_inc(v_turned, 1)
                    pending += [pick_k, turn_v]
                elif ph.kind == "q":
                    t_bank, o_views, swap_bank = q_places(ph)

                    def project_q(m, half=None):
                        pe.wait_ge(drained, g0 + max(m - 1, 0))
                        ks = None if half is None else range(half * DT // 2, (half + 1) * DT // 2)
                        group(b0 + m, b0 + m, g0 + m, g0 + m % 2, DT, hg_hi, hg_lo, tile,
                              ready=hg_ready if m == 0 else None, part=ks)

                    def project_o(o, *ks):
                        if o == 3:
                            pe.wait_ge(q_step, 3 * DT)
                        pe.wait_ge(act_split, ph.tile0 + 4 * (ks[-1] // 2) + 4)
                        group(b0 + DT + o, b0 + DT + o, g0 + DT, g0 + DT + o, DT, act_hi, act_lo, tile, part=ks)

                    def swap_q(m):
                        pe.wait_ge(drained, g0 + m + 1)
                        if m:
                            pe.wait_ge(q_step, 3 * m - 1)
                        nc.tensor.matmul(swap_bank(m)[:, :], tab[:, T_SWAP:T_SWAP + P], tmp[:, m % 2, :],
                                         start=True, stop=True).then_inc(q_swapped, 1)

                    def score(n):
                        pair, cp = n // 4, n % 4
                        pe.wait_ge(q_split, 2 * pair + 2)
                        if n >= 2:
                            pe.wait_ge(exped, n - 1)
                        for u in range(2):
                            c = 2 * cp + u
                            dst = bank[4 + n % 2][:, 2 * u * P:2 * (u + 1) * P]
                            if c == 0:
                                nc.tensor.matmul(dst, ones_r[:, :], mask[:, :], start=True, stop=False)
                            for step, (q, k) in enumerate(((q_hi, k_hi), (q_hi, k_lo), (q_lo, k_hi))):
                                mm = nc.tensor.matmul(dst, q[:, pair % 2, c, :, :].rearrange("p t q -> p (t q)"),
                                                      k[:, pair // 2, :, c * CHUNK:c * CHUNK + P],
                                                      start=(step == 0 and c > 0), stop=(step == 2))
                        mm.then_inc(scored, 1)

                    def turn_p(n):
                        pe.wait_ge(probs_ready, n + 1)
                        if n >= 2:
                            pe.wait_ge(p_split, n - 1)
                        for u in range(4):
                            mm = nc.tensor.transpose(t_bank(n)[:, u * P:(u + 1) * P], prob[:, n % 2, u, :], ident)
                        mm.then_inc(p_turned, 1)

                    def weigh_v(n):
                        pair, cp = n // 4, n % 4
                        pe.wait_ge(p_split, n + 1)
                        if n:
                            pe.wait_ge(act_split, ph.tile0 + n)
                        for u in range(2):
                            dst = bank[7][:, 2 * u * P:2 * (u + 1) * P]
                            for step, (v, p) in enumerate(((v_hi, pt_hi), (v_hi, pt_lo), (v_lo, pt_hi))):
                                mm = nc.tensor.matmul(
                                    dst, v[:, 2 * cp + u, pair // 2, :, :].rearrange("p a d -> p (a d)"),
                                    p[:, n % 2, 2 * u:2 * u + 2, :], start=(step == 0), stop=(step == 2))
                        mm.then_inc(pv_done, 1)

                    project_q(0)
                    pending.pop(0)()
                    project_q(1)
                    project_q(2, 0)
                    swap_q(0)
                    project_q(2, 1)
                    swap_q(1)
                    project_q(3, 0)
                    pe.wait_ge(k_split, KV_HEADS)
                    pe.wait_ge(v_split, 2)
                    pe.wait_ge(kv_pads, 6)
                    pe.wait_ge(masks_set, 3)
                    filler = {-2: (project_q, 3, 1), -1: (project_q, 4, 0), 0: (project_q, 4, 1)}
                    filler.update({2 * m - 8 + half: (project_q, m, half) for m in range(5, DT) for half in range(2)})
                    filler.update({8: (project_o, 0, 0, 1), 9: (project_o, 1, 0, 1), 10: (project_o, 0, 2, 3),
                                   11: (project_o, 1, 2, 3), 12: (project_o, 3, 0, 1), 13: (project_o, 3, 2, 3),
                                   14: (project_o, 0, 4, 5), 15: (project_o, 1, 4, 5), 16: (project_o, 3, 4, 5)})
                    for s in attention_steps:
                        m, part = tile_in_work(s)
                        if s + 2 < BATCHES:
                            score(s + 2)
                        if s in filler:
                            filler[s][0](*filler[s][1:])
                        if 0 <= s + 1 < BATCHES:
                            turn_p(s + 1)
                        if m < DT and part == 0:
                            swap_q(m)
                        if 0 <= s < BATCHES:
                            weigh_v(s)
                elif ph.kind == "final":
                    def split_ready(k):
                        pe.wait_ge(act_split, ph.tile0 - ph.kt + k + 1)
                    for o in range(DT):
                        group(b0 + o, b0 + o, g0 + o, g0 + o, ph.kt, act_hi, act_lo, tile,
                              ready=split_ready if o == 0 else None)
                    pe.wait_ge(sq_summed, 9 * ph.norm0 + DT)
                    pe.wait_ge(squared, DT * (ph.norm0 + 1))
                    for c in range(S // P):
                        for last, sums in enumerate((sqsum[:, :], sq[:, (DT - 1) % 2, :])):
                            mm = nc.tensor.matmul(bank[4][:, c:c + 1], sums[:, c * P:(c + 1) * P], ones[:, 0:1],
                                                  start=not last, stop=bool(last))
                    mm.then_inc(rms_summed, 1)
                    pe.wait_ge(rstd_ready, ph.norm0 + 2)
                    nc.tensor.matmul(bank[5][:, :], ones, tmp[:, 0, :], start=True, stop=True).then_inc(rms_summed, 1)


LRU_CONST_STEPS = 25


def weight_stream(inputs):
    phases = plan()
    stream = np.zeros((phases[-1].block0 + phases[-1].n_blocks, P, BLK), np.float32)

    def put(block, w, c):
        kt = w.shape[0] // P
        stream[block, :, 0:kt * P] = w[:, c:c + P].reshape(kt, P, P).transpose(1, 0, 2).reshape(P, kt * P)

    for ph in phases:
        if ph.kind == "gu":
            w = inputs["ffn_w_gu"][ph.layer, ph.which]
            for n in range(ph.n_blocks):
                put(ph.block0 + n, w, (ph.first + n // 2) * P + (F if n % 2 else 0))
        elif ph.kind in ("down", "final"):
            w = inputs["ffn_w_down"][ph.layer, ph.which, ph.first * P:(ph.first + ph.kt) * P]
            for n in range(ph.n_blocks):
                put(ph.block0 + n, w, n * P)
        elif ph.kind == "gates":
            for n in range(ph.n_blocks):
                w = inputs["lru_gate_w"][0, :, n]
                stream[ph.block0 + n] = w.reshape(2, 2, P, 2 * P).transpose(2, 0, 1, 3).reshape(P, BLK)
        elif ph.n_blocks:
            w = {"xb": lambda: inputs["lru_w_in"][0][:, 0:D], "yb": lambda: inputs["lru_w_in"][0][:, D:2 * D],
                 "kv": lambda: inputs["w_kv"], "q": lambda: inputs["attn_w_q"][0],
                 "out": lambda: inputs[ph.weight][0]}[ph.kind]()
            for n in range(ph.n_blocks):
                put(ph.block0 + n, w, n * P)
    return stream


def parameter_columns(inputs):
    names = ("ffn_norm", "mix_norm", "kv_norm", "final_norm", "lru_conv_w", "lru_conv_b", "lru_gate_b", "lru_a_param")
    cols = np.concatenate([inputs[k].reshape(-1, P) for k in names]).T
    heads = inputs["attn_sinks"].reshape(4, 2, 2)
    sinks = np.repeat(heads.transpose(1, 0, 2).reshape(2, 8), P // 2, axis=0)
    return np.ascontiguousarray(np.concatenate([cols, sinks], axis=1))


def kernel(**inputs):
    import concourse.bacc as _bacc
    from concourse.bass_utils import run_bass_kernel_spmd as _run

    inputs = {k: np.asarray(v) for k, v in inputs.items()}
    nc = _bacc.Bacc("TRN2", target_bir_lowering=False, num_devices=1)
    arrays, args = {}, []
    for name, a in (("x_dram", np.ascontiguousarray(inputs["x"][0].T.reshape(DT, P, S).transpose(1, 0, 2))),
                    ("params_dram", parameter_columns(inputs)),
                    ("weights_dram", weight_stream(inputs)),
                    ("tables_dram", shape_tables())):
        arrays[name] = a
        args.append(nc.dram_tensor(name, a.shape, F32, kind="ExternalInput").ap())
    args.append(nc.dram_tensor("out_dram", (P, DT, S), F32, kind="ExternalOutput").ap())
    trunk_program(nc, *args)
    r = _run(nc, [arrays], core_ids=[0])
    return np.ascontiguousarray(r.results[0]["out_dram"].transpose(1, 0, 2).reshape(D, S).T[None])
```
